# Optimizing a Trainium2 kernel written in Bass

```python
import jax, jax.numpy as jnp
from jax import lax
import numpy as np

D_MODEL = 2048
BATCH = 1
SEQ = 128
DEPTH = 1
DEC_BATCH = 1
DEC_SEQ = 512
PAST_LEN = 128

GRID_W = 64
D_A = 1024
H_B = 32
HEAD_DIM = 64
D_B = H_B * HEAD_DIM
LORA_W = 96
LORA_A = 96
LORA_G = 256
N_DIR = 2
PEER_HEADS = 8
N_KEYS = 128
N_EXPERTS = N_KEYS * N_KEYS
D_KEY = 256
HALF_KEY = D_KEY // 2
PEER_TOPK = 16
TOKEN_BLOCK = 128
RMS_EPS = 1e-6
GN_EPS = 64e-5
IN_WIDTHS = (D_A, D_A, D_A, D_B, D_B, D_B, LORA_W, LORA_W, LORA_A, LORA_A, LORA_G, D_MODEL, D_MODEL)
D_IN = 3 * D_A + 3 * D_B + 2 * LORA_W + 2 * LORA_A + LORA_G + 2 * D_MODEL

kernel_name = "hybrid_conv_rwkv7_peer_prefix_dit"

def _rmsnorm(x, g):
    xf = x.astype(jnp.float32)
    y = xf * lax.rsqrt(jnp.mean(xf * xf, axis=-1, keepdims=True) + RMS_EPS)
    return (y * g.astype(jnp.float32)).astype(x.dtype)

def _conv3(x, w, axis):
    n = x.shape[axis]
    pad = [(0, 0)] * x.ndim
    pad[axis] = (1, 1)
    xp = jnp.pad(x, pad)
    prev = lax.slice_in_dim(xp, 0, n, axis=axis)
    nxt = lax.slice_in_dim(xp, 2, n + 2, axis=axis)
    return w[0] * prev + w[1] * x + w[2] * nxt

def _short_conv(u_b, u_c, u_x, conv_w, w_out_a, rows):
    z = u_c * u_x
    if rows is None:
        zc = _conv3(z, conv_w, axis=1)
    else:
        b_, t_, ch = z.shape
        half = ch // 2
        zg = z.reshape(b_, rows, GRID_W, ch)
        zh = _conv3(zg[..., :half], conv_w[:, :half], axis=2)
        zv = _conv3(zg[..., half:], conv_w[:, half:], axis=1)
        zc = jnp.concatenate([zh, zv], axis=-1).reshape(b_, t_, ch)
    return (u_b * zc) @ w_out_a

def _wkv_scan(r, w, k, v, a_vec, b_vec, S0, reverse):
    def step(S, inp):
        r_t, w_t, k_t, v_t, a_t, b_t = inp
        sa = jnp.einsum('bhvk,bhk->bhv', S, a_t)
        S = S * w_t[:, :, None, :] + sa[..., None] * b_t[:, :, None, :] + v_t[..., None] * k_t[:, :, None, :]
        return S, jnp.einsum('bhvk,bhk->bhv', S, r_t)
    xs = tuple(jnp.moveaxis(t, 1, 0) for t in (r, w, k, v, a_vec, b_vec))
    S_fin, out = lax.scan(step, S0, xs, reverse=reverse)
    return jnp.moveaxis(out, 0, 1), S_fin

def _rwkv7(r, k, v, wd, ad, gd, S0, w0, w_up, a0, a_up, g_up, k_k, k_a, r_k, ln_g, ln_b, w_o):
    b_, t_, _ = r.shape
    heads = lambda t: t.reshape(b_, t_, H_B, HEAD_DIM)
    rh, kh, vh = heads(r), heads(k), heads(v)
    kk = (kh * k_k.reshape(H_B, HEAD_DIM)).astype(jnp.float32)
    kk = (kk * lax.rsqrt(jnp.sum(kk * kk, axis=-1, keepdims=True) + 1e-12)).astype(r.dtype)
    S0 = S0.astype(r.dtype)
    outs, bonus, finals = [], [], []
    for d in range(N_DIR):
        w_log = -jax.nn.softplus(-(w0[d] + jnp.tanh(wd[d]) @ w_up[d])) - 0.5
        decay = heads(jnp.exp(-jnp.exp(w_log)))
        a = heads(jax.nn.sigmoid(a0[d] + ad[d] @ a_up[d]))
        kd = kh * (1 + (a - 1) * k_a.reshape(H_B, HEAD_DIM))
        o, S_fin = _wkv_scan(rh, decay, kd, vh, -kk, kk * a, S0[:, d], reverse=(d == 1))
        outs.append(o)
        finals.append(S_fin)
        bonus.append(jnp.sum(rh * kd * r_k, axis=-1, keepdims=True) * vh)
    o = (outs[0] + outs[1]).astype(jnp.float32)
    mu = jnp.mean(o, axis=-1, keepdims=True)
    var = jnp.mean(jnp.square(o - mu), axis=-1, keepdims=True)
    o = ((o - mu) * lax.rsqrt(var + GN_EPS)).astype(r.dtype)
    o = o * ln_g.reshape(H_B, HEAD_DIM) + ln_b.reshape(H_B, HEAD_DIM)
    o = o + bonus[0] + bonus[1]
    g = jax.nn.sigmoid(gd) @ g_up
    y = (o.reshape(b_, t_, D_B) * g) @ w_o
    return y, jnp.stack(finals, axis=1)

def _peer(h, w_q, sub_keys, u_tab, v_tab):
    b_, t_, dm = h.shape
    hb = h.reshape(-1, TOKEN_BLOCK, dm)

    def block(hx):
        q = (hx @ w_q).reshape(TOKEN_BLOCK, PEER_HEADS, 2, HALF_KEY)
        s = jnp.einsum('thpd,phkd->thpk', q, sub_keys)
        s1, i1 = lax.top_k(s[:, :, 0], PEER_TOPK)
        s2, i2 = lax.top_k(s[:, :, 1], PEER_TOPK)
        cand = (s1[..., :, None] + s2[..., None, :]).reshape(TOKEN_BLOCK, PEER_HEADS, PEER_TOPK * PEER_TOPK)
        ids = (i1[..., :, None] * N_KEYS + i2[..., None, :]).reshape(TOKEN_BLOCK, PEER_HEADS, PEER_TOPK * PEER_TOPK)
        top_s, pos = lax.top_k(cand, PEER_TOPK)
        eid = jnp.take_along_axis(ids, pos, axis=-1)
        g = jax.nn.softmax(top_s.astype(jnp.float32), axis=-1).astype(hx.dtype)
        act = jax.nn.gelu(jnp.einsum('td,thkd->thk', hx, u_tab[eid]))
        return jnp.einsum('thk,thkd->td', g * act, v_tab[eid])

    return lax.map(block, hb).reshape(b_, t_, dm)

def _layer(x, mod, S0, rows, norm1_g, norm2_g, w_in, conv_w, w_out_a, w0, w_up, a0, a_up, g_up,
           k_k, k_a, r_k, ln_g, ln_b, w_o, w_mix, w_q, sub_keys, u_tab, v_tab):
    sh1, sc1, gt1, sh2, sc2, gt2 = jnp.split(mod, 6, axis=-1)
    h = _rmsnorm(x, norm1_g) * (1 + sc1) + sh1
    cuts = [int(i) for i in np.cumsum(IN_WIDTHS)[:-1]]
    (u_b, u_c, u_x, r, k, v, wd_f, wd_b, ad_f, ad_b, gd, gate_a, gate_b) = jnp.split(h @ w_in, cuts, axis=-1)
    y_a = _short_conv(u_b, u_c, u_x, conv_w, w_out_a, rows)
    y_b, S_fin = _rwkv7(r, k, v, (wd_f, wd_b), (ad_f, ad_b), gd, S0, w0, w_up, a0, a_up, g_up,
                        k_k, k_a, r_k, ln_g, ln_b, w_o)
    merged = jax.nn.sigmoid(gate_a) * y_a + jax.nn.sigmoid(gate_b) * y_b
    x = x + gt1 * (merged @ w_mix)
    h2 = _rmsnorm(x, norm2_g) * (1 + sc2) + sh2
    x = x + gt2 * _peer(h2, w_q, sub_keys, u_tab, v_tab)
    return x, S_fin

def setup_inputs(seed: int = 0) -> dict:
    key = jax.random.key(seed)
    ks = iter(jax.random.split(key, 32))
    nrm = lambda shape, s: jax.random.normal(next(ks), shape, jnp.float32) * s
    L = DEPTH
    return {
        "x_prompt": nrm((BATCH, SEQ, D_MODEL), 1.0),
        "x_sample": nrm((DEC_BATCH, DEC_SEQ, D_MODEL), 1.0),
        "state_rwkv": nrm((DEC_BATCH, L, N_DIR, H_B, HEAD_DIM, HEAD_DIM), 0.5),
        "c": nrm((DEC_BATCH, D_MODEL), 1.0),
        "c_ctx": nrm((D_MODEL,), 1.0),
        "w_ada": nrm((L, D_MODEL, 6 * D_MODEL), 0.5 * D_MODEL ** -0.5),
        "b_ada": nrm((L, 6 * D_MODEL), 0.01),
        "norm1_g": 1.0 + nrm((L, D_MODEL), 0.1),
        "norm2_g": 1.0 + nrm((L, D_MODEL), 0.1),
        "w_in": nrm((L, D_MODEL, D_IN), D_MODEL ** -0.5),
        "conv_w": nrm((L, 3, D_A), 0.5),
        "w_out_a": nrm((L, D_A, D_MODEL), D_A ** -0.5),
        "w0": nrm((L, N_DIR, D_B), 1.0),
        "w_up": nrm((L, N_DIR, LORA_W, D_B), 0.5 * LORA_W ** -0.5),
        "a0": nrm((L, N_DIR, D_B), 0.1),
        "a_up": nrm((L, N_DIR, LORA_A, D_B), 0.5 * LORA_A ** -0.5),
        "g_up": nrm((L, LORA_G, D_B), LORA_G ** -0.5),
        "k_k": 0.85 + nrm((L, D_B), 0.05),
        "k_a": 1.0 + nrm((L, D_B), 0.05),
        "r_k": nrm((L, H_B, HEAD_DIM), 0.1),
        "ln_g": 1.0 + nrm((L, D_B), 0.1),
        "ln_b": nrm((L, D_B), 0.01),
        "w_o": nrm((L, D_B, D_MODEL), D_B ** -0.5),
        "w_mix": nrm((L, D_MODEL, D_MODEL), D_MODEL ** -0.5),
        "w_q": nrm((L, D_MODEL, PEER_HEADS * D_KEY), D_MODEL ** -0.5),
        "sub_keys": nrm((L, 2, PEER_HEADS, N_KEYS, HALF_KEY), HALF_KEY ** -0.5),
        "u_tab": nrm((L, N_EXPERTS, D_MODEL), D_MODEL ** -0.5),
        "v_tab": nrm((L, N_EXPERTS, D_MODEL), 0.5),
        "final_g": 1.0 + nrm((D_MODEL,), 0.1),
    }

def reference(x_prompt, x_sample, state_rwkv, c, c_ctx, w_ada, b_ada, norm1_g, norm2_g, w_in, conv_w,
              w_out_a, w0, w_up, a0, a_up, g_up, k_k, k_a, r_k, ln_g, ln_b, w_o, w_mix, w_q, sub_keys,
              u_tab, v_tab, final_g):
    rows = x_sample.shape[1] // GRID_W
    xp, xs = x_prompt, x_sample
    new_states = []
    for l in range(DEPTH):
        lp = (norm1_g[l], norm2_g[l], w_in[l], conv_w[l], w_out_a[l], w0[l], w_up[l], a0[l], a_up[l],
              g_up[l], k_k[l], k_a[l], r_k[l], ln_g[l], ln_b[l], w_o[l], w_mix[l], w_q[l], sub_keys[l],
              u_tab[l], v_tab[l])
        mod_ctx = (jax.nn.silu(c_ctx) @ w_ada[l] + b_ada[l])[None, None, :]
        mod_lat = (jax.nn.silu(c) @ w_ada[l] + b_ada[l])[:, None, :]
        S0_ctx = jnp.zeros((xp.shape[0], N_DIR, H_B, HEAD_DIM, HEAD_DIM), xp.dtype)
        xp, S_ctx = _layer(xp, mod_ctx, S0_ctx, None, *lp)
        new_states.append(S_ctx)
        xs, _ = _layer(xs, mod_lat, state_rwkv[:, l], rows, *lp)
    y_prompt = _rmsnorm(xp, final_g)
    y_sample = _rmsnorm(xs, final_g)
    new_state_rwkv = jnp.stack(new_states, axis=1)
    return (y_prompt, y_sample, new_state_rwkv)


_drawn_inputs = setup_inputs


def setup_inputs(seed=0):
    import zlib

    import numpy as np

    out = dict(_drawn_inputs(seed))
    spreads = {}
    factors = {'state_rwkv': 8.0, 'b_ada': 2.871, 'k_k': 26.677, 'ln_g': 4.888, 'ln_b': 47.477}
    for name, (base, spread) in spreads.items():
        noise = np.random.default_rng([zlib.crc32(name.encode()), seed]).standard_normal(out[name].shape)
        drawn = base * np.exp(spread * noise) if base else spread * noise
        out[name] = __import__('jax').numpy.asarray(drawn.astype(out[name].dtype))
    for name, factor in factors.items():
        out[name] = (out[name] * factor).astype(out[name].dtype)
    return out
```

```python
from contextlib import ExitStack

import numpy as np

import concourse.bass as bass
from concourse import mybir

F32 = mybir.dt.float32
F32R = mybir.dt.float32r
U32 = mybir.dt.uint32
ALU = mybir.AluOpType
ACT = mybir.ActivationFunctionType
AX = mybir.AxisListType

P = 128
D = 2048
KT = D // P
T_PROMPT, T_SAMPLE = 128, 512
NT = T_PROMPT + T_SAMPLE
NB = NT // P
HALF = NT // 2
GRID_W = 64
D_A = 1024
ZT = D_A // P
HEAD = 64
NJ = D // P
LORA = 96
PEER_HEADS = 8
N_KEYS = 128
TOPK = 16
UK = 8
E_TILES = N_KEYS
E_GROUP = 8
RMS_EPS, GN_EPS, KK_EPS = 1e-6, 64e-5, 1e-12
DECAY_RATE = float(np.exp(-0.5))
GROUPS = ((0, 0, T_PROMPT), (1, T_PROMPT, NT))


def halves(ap):
    return ap.rearrange("p (a n) -> p a n", a=2)


def blocks(ap):
    return ap.rearrange("p (b t) -> p b t", b=NB)


class WeightStream:

    def __init__(self, nc, ctx, name, dram):
        self.dram = dram
        self.raw = ctx.enter_context(nc.sbuf_tensor(name + "_raw", [P, 2, UK * P], F32))
        self.hi = ctx.enter_context(nc.sbuf_tensor(name + "_hi", [P, 2, UK * P], F32R))
        self.lo = ctx.enter_context(nc.sbuf_tensor(name + "_lo", [P, 2, UK * P], F32R))
        self.loaded = [nc.alloc_semaphore(f"{name}_loaded{s}") for s in range(2)]
        self.hi_done = nc.alloc_semaphore(name + "_hi_done")
        self.lo_done = nc.alloc_semaphore(name + "_lo_done")
        self.used = nc.alloc_semaphore(name + "_used")

    def load(self, sync, r, slot):
        if not is_zero(r):
            sync.wait_ge(self.lo_done, 2 * r + slot - 1)
        sync.dma_start(self.raw[:, slot, :], row(self.dram, 2 * r + slot)).then_inc(self.loaded[slot], 16)

    def split_hi(self, act, r, slot):
        act.wait_ge(self.loaded[slot], 16 * r + 16)
        if not is_zero(r):
            act.wait_ge(self.used, 2 * r + slot - 1)
        act.activation(self.hi[:, slot, :], self.raw[:, slot, :], ACT.Copy).then_inc(self.hi_done, 1)

    def split_lo(self, dve, r, slot):
        dve.wait_ge(self.hi_done, 2 * r + slot + 1)
        dve.tensor_tensor(self.lo[:, slot, :], self.raw[:, slot, :], self.hi[:, slot, :].bitcast(F32),
                          ALU.subtract).then_inc(self.lo_done, 1)

    def products(self, pe, r, slot, out, x_hi, x_lo, k0, start, stop):
        pe.wait_ge(self.lo_done, 2 * r + slot + 1)
        for k in range(UK):
            w_hi = self.hi[:, slot, k * P:(k + 1) * P]
            w_lo = self.lo[:, slot, k * P:(k + 1) * P]
            for n, (w, x) in enumerate(((w_hi, x_hi), (w_hi, x_lo), (w_lo, x_hi))):
                for a in range(2):
                    last = pe.matmul(out[:, a, 0:HALF], w, x[:, k0 + k, a * HALF:(a + 1) * HALF],
                                     start=(start and k == 0 and n == 0),
                                     stop=(stop and k == UK - 1 and n == 2))
        last.then_inc(self.used, 1)


def is_zero(i):
    return isinstance(i, int) and i == 0


def at(i):
    return slice(i, i + 1) if isinstance(i, int) else bass.ds(i, 1)


def row(dram, i):
    return dram[i]


def full_product(ws, pe, r, out, x_hi, x_lo):
    ws.products(pe, r, 0, out, x_hi, x_lo, 0, True, False)
    ws.products(pe, r, 1, out, x_hi, x_lo, UK, False, True)


def modulation(nc, io, mod):
    M = 6 * KT
    with ExitStack() as ctx:
        sb = lambda name, shape: ctx.enter_context(nc.sbuf_tensor(name, shape, F32))
        sem = lambda name: nc.alloc_semaphore(name)
        ada = sb("ada", [P, 4, KT * P])
        cond, sig = sb("cond", [P, KT, 2]), sb("cond_sig", [P, KT, 2])
        bias = sb("b_ada", [P, M])
        ps = ctx.enter_context(nc.psum_tensor("mod_ps", [P, 2, 512], F32))
        small_loaded, sig_done = sem("m_small"), sem("m_sig")
        ada_loaded = [sem(f"m_ada{s}") for s in range(4)]
        cond_done, tile_done, mod_done = sem("m_cond"), sem("m_tile"), sem("m_done")
        block = ctx.enter_context(nc.Block())

        @block.sync
        def _(sync):
            sync.dma_start(cond[:], io["c_pair"]).then_inc(small_loaded, 16)
            sync.dma_start(bias[:], io["b_ada"]).then_inc(small_loaded, 16)
            for s in range(4):
                sync.dma_start(ada[:, s, :], io["w_ada"][s]).then_inc(ada_loaded[s], 16)
            with sync.Fori(1, M // 4) as i:
                for s in range(4):
                    sync.wait_ge(tile_done, 4 * i + s - 3)
                    sync.dma_start(ada[:, s, :],
                                   row(io["w_ada"], 4 * i + s)).then_inc(ada_loaded[s], 16)

        @block.scalar
        def _(act):
            act.wait_ge(small_loaded, 32)
            act.activation(sig[:], cond[:], ACT.Sigmoid).then_inc(sig_done, 1)

        @block.vector
        def _(dve):
            dve.wait_ge(small_loaded, 32)
            dve.wait_ge(sig_done, 1)
            dve.tensor_tensor(cond[:], cond[:], sig[:], ALU.mult).then_inc(cond_done, 1)
            with dve.Fori(0, M // 8) as i:
                for half in range(2):
                    dve.wait_ge(tile_done, 8 * i + 4 * half + 4)
                    dve.tensor_tensor(mod[:, bass.ds(8 * i + 4 * half, 4), :],
                                      ps[:, half, 0:8].rearrange("p (m g) -> p m g", g=2),
                                      bias[:, bass.ds(8 * i + 4 * half, 4), None].to_broadcast((P, 4, 2)),
                                      ALU.add).then_inc(mod_done, 1)

        @block.tensor
        def _(pe):
            def body(i, first):
                for s in range(8):
                    if s % 4 == 0 and not first:
                        pe.wait_ge(mod_done, 2 * i + s // 4 - 1)
                    pe.wait_ge(ada_loaded[s % 4], 32 * i + 16 * (s // 4) + 16)
                    for k in range(KT):
                        last = pe.matmul(ps[:, s // 4, 2 * (s % 4):2 * (s % 4) + 2],
                                         ada[:, s % 4, k * P:(k + 1) * P], cond[:, k, :],
                                         start=(k == 0), stop=(k == KT - 1))
                    last.then_inc(tile_done, 1)
            pe.wait_ge(cond_done, 1)
            body(0, True)
            with pe.Fori(1, M // 8) as i:
                body(i, False)


def norm(nc, io, name, x, gain, scale, shift, out_hi=None, out_lo=None, x_dram=None, out_dram=None):
    with ExitStack() as ctx:
        sb = lambda n, shape: ctx.enter_context(nc.sbuf_tensor(name + n, shape, F32))
        sem = lambda n: nc.alloc_semaphore(name + n)
        ones, g, amp, eps = sb("ones", [P, P]), sb("gain", [P, KT]), sb("amp", [P, KT, 2]), sb("eps", [P, 3])
        sq, rstd, out = sb("sq", [P, 2, NT]), sb("rstd", [P, NT]), sb("out", [P, 2, NT])
        ps = ctx.enter_context(nc.psum_tensor(name + "ps", [P, 2, 512], F32))
        loaded, x_loaded, squared, summed, rooted = (sem(s) for s in ("ld", "xld", "sq_d", "sum", "root"))
        amp_done, rstd_done, scaled, shifted, hi_done, lo_done, *stored = (
            sem(s) for s in ("amp_d", "rstd_d", "scaled", "shift", "hi_d", "lo_d", "stored0", "stored1"))
        block = ctx.enter_context(nc.Block())

        @block.sync
        def _(sync):
            sync.dma_start(g[:], gain).then_inc(loaded, 16)
            sync.dma_start(ones[:], io["ones"]).then_inc(loaded, 16)
            sync.dma_start(eps[:], io["eps"]).then_inc(loaded, 16)
            if x_dram is not None:
                for k in range(KT):
                    sync.dma_start(x[:, k, :], x_dram[k]).then_inc(x_loaded, 16)
            if out_dram is not None:
                for k in range(KT):
                    sync.wait_ge(shifted, k + 1)
                    sync.dma_start(out_dram[k], out[:, k % 2, :]).then_inc(stored[k % 2], 16)
                for slot in range(2):
                    sync.wait_ge(stored[slot], 16 * (KT // 2))

        @block.scalar
        def _(act):
            for k in range(KT):
                if x_dram is not None:
                    act.wait_ge(x_loaded, 16 * KT)
                if k >= 2:
                    act.wait_ge(summed, k - 1)
                act.activation(sq[:, k % 2, :], x[:, k, :], ACT.Square).then_inc(squared, 1)
            act.wait_ge(loaded, 48)
            act.wait_ge(summed, KT)
            act.activation(halves(rstd[:]), ps[:, :, 0:HALF], ACT.Sqrt, scale=1.0 / D,
                           bias=eps[:, 0:1]).then_inc(rooted, 1)
            if out_hi is not None:
                for k in range(KT):
                    act.wait_ge(shifted, 2 * (k + 1))
                    act.activation(out_hi[:, k, :], out[:, k % 2, :], ACT.Copy).then_inc(hi_done, 1)

        @block.tensor
        def _(pe):
            pe.wait_ge(loaded, 48)
            for k in range(KT):
                pe.wait_ge(squared, k + 1)
                for a in range(2):
                    last = pe.matmul(ps[:, a, 0:HALF], ones[:], sq[:, k % 2, a * HALF:(a + 1) * HALF],
                                     start=(k == 0), stop=(k == KT - 1))
                last.then_inc(summed, 1)

        def split_lo(dve, k):
            dve.wait_ge(hi_done, k + 1)
            dve.tensor_tensor(out_lo[:, k, :], out[:, k % 2, :], out_hi[:, k, :].bitcast(F32),
                              ALU.subtract).then_inc(lo_done, 1)

        @block.vector
        def _(dve):
            dve.wait_ge(loaded, 48)
            if scale is not None:
                dve.tensor_scalar(amp[:], scale, 1.0, None, ALU.add).then_inc(amp_done, 1)
                dve.wait_ge(amp_done, 1)
                dve.tensor_tensor(amp[:], amp[:], g[:, :, None].to_broadcast((P, KT, 2)),
                                  ALU.mult).then_inc(amp_done, 1)
                dve.wait_ge(amp_done, 2)
            dve.wait_ge(rooted, 1)
            dve.reciprocal(rstd[:], rstd[:]).then_inc(rstd_done, 1)
            dve.wait_ge(rstd_done, 1)
            for k in range(KT):
                if out_dram is not None:
                    if k >= 2:
                        dve.wait_ge(stored[k % 2], 16 * (k // 2))
                    dve.tensor_tensor(out[:, k % 2, :], x[:, k, :], rstd[:], ALU.mult).then_inc(scaled, 1)
                    dve.wait_ge(scaled, k + 1)
                    dve.tensor_scalar(out[:, k % 2, :], out[:, k % 2, :], g[:, k:k + 1], None,
                                      ALU.mult).then_inc(shifted, 1)
                    continue
                if k >= 2:
                    dve.wait_ge(lo_done, k - 1)
                dve.tensor_tensor(out[:, k % 2, :], x[:, k, :], rstd[:], ALU.mult).then_inc(scaled, 1)
                dve.wait_ge(scaled, k + 1)
                for col, t0, t1 in GROUPS:
                    dve.tensor_scalar(out[:, k % 2, t0:t1], out[:, k % 2, t0:t1], amp[:, k, col:col + 1],
                                      shift[:, k, col:col + 1], ALU.mult, ALU.add).then_inc(shifted, 1)
                if k >= 1:
                    split_lo(dve, k - 1)
            if out_hi is not None:
                split_lo(dve, KT - 1)


def gemm_loop(ws, sync, rounds):
    for slot in range(2):
        ws.load(sync, 0, slot)
    with sync.Fori(1, rounds) as r:
        for slot in range(2):
            ws.load(sync, r, slot)


def conv_branch(nc, io, h_hi, h_lo, z_hi, z_lo):
    with ExitStack() as ctx:
        sb = lambda n, shape: ctx.enter_context(nc.sbuf_tensor(n, shape, F32))
        sem = lambda n: nc.alloc_semaphore(n)
        ws = WeightStream(nc, ctx, "wa", io["w_conv"])
        ps = ctx.enter_context(nc.psum_tensor("a_ps", [P, 3, 2, 512], F32))
        c, z, zc = sb("a_c", [P, NT]), sb("a_z", [P, NT]), sb("a_zc", [P, NT])
        taps = sb("a_taps", [P, ZT, 3])
        taps_loaded, out_done, c_copied = sem("a_taps_l"), sem("a_out"), sem("a_c_d")
        z_done, conv_done, hi_done, lo_done = sem("a_z_d"), sem("a_conv"), sem("a_hi"), sem("a_lo")
        block = ctx.enter_context(nc.Block())

        @block.sync
        def _(sync):
            sync.dma_start(taps[:], io["conv_w"]).then_inc(taps_loaded, 16)
            gemm_loop(ws, sync, 3 * ZT)

        @block.tensor
        def _(pe):
            def body(j, first):
                for s in range(3):
                    if not first:
                        pe.wait_ge(*((c_copied, j), (z_done, j), (conv_done, CONV_STEPS * j))[s])
                    full_product(ws, pe, 3 * j + s, ps[:, s], h_hi, h_lo)
            body(0, True)
            with pe.Fori(1, ZT) as j:
                body(j, False)

        @block.scalar
        def _(act):
            def body(j, first, last):
                for s in range(3):
                    if not (last and s == 2):
                        for slot in range(2):
                            ws.split_hi(act, 3 * j + s + 1, slot)
                    if s == 0:
                        act.wait_ge(ws.used, 6 * j + 2)
                        if not first:
                            act.wait_ge(z_done, j)
                        act.activation(halves(c[:]), ps[:, 0, :, 0:HALF], ACT.Copy).then_inc(c_copied, 1)
                act.wait_ge(conv_done, CONV_STEPS * j + CONV_STEPS)
                act.activation(z_hi[:, at(j), :], zc[:, None, :], ACT.Copy).then_inc(hi_done, 1)
            for slot in range(2):
                ws.split_hi(act, 0, slot)
            body(0, True, False)
            with act.Fori(1, ZT - 1) as j:
                body(j, False, False)
            body(ZT - 1, False, True)

        @block.vector
        def _(dve):
            def body(j, first, last, along_rows):
                for slot in range(2):
                    ws.split_lo(dve, 3 * j + 1, slot)
                for slot in range(2):
                    ws.split_lo(dve, 3 * j + 2, slot)
                dve.wait_ge(c_copied, j + 1)
                dve.wait_ge(ws.used, 6 * j + 4)
                dve.tensor_tensor(halves(z[:]), halves(c[:]), ps[:, 1, :, 0:HALF], ALU.mult
                                  ).then_inc(z_done, 1)
                dve.wait_ge(z_done, j + 1)
                if not first:
                    dve.wait_ge(lo_done, j)
                tap = lambda n: taps[:, at(j), n:n + 1].rearrange("p a n -> p (a n)")
                dve.tensor_scalar(zc[:], z[:], tap(1), None, ALU.mult).then_inc(conv_done, 1)
                step = 1
                for n, dst, src in shifted_views(zc, z, along_rows):
                    dve.wait_ge(conv_done, CONV_STEPS * j + step)
                    dve.scalar_tensor_tensor(dst, src, tap(n), dst, ALU.mult, ALU.add
                                             ).then_inc(conv_done, 1)
                    step += 1
                if not last:
                    for slot in range(2):
                        ws.split_lo(dve, 3 * j + 3, slot)
                dve.wait_ge(conv_done, CONV_STEPS * j + step)
                dve.wait_ge(ws.used, 6 * j + 6)
                dve.tensor_tensor(halves(zc[:]), halves(zc[:]), ps[:, 2, :, 0:HALF], ALU.mult
                                  ).then_inc(conv_done, 1)
                dve.wait_ge(hi_done, j + 1)
                dve.tensor_tensor(z_lo[:, at(j), :], zc[:, None, :], z_hi[:, at(j), :].bitcast(F32),
                                  ALU.subtract).then_inc(lo_done, 1)
            dve.wait_ge(taps_loaded, 16)
            for slot in range(2):
                ws.split_lo(dve, 0, slot)
            body(0, True, False, True)
            with dve.Fori(1, ZT // 2) as j:
                body(j, False, False, True)
            with dve.Fori(ZT // 2, ZT - 1) as j:
                body(j, False, False, False)
            body(ZT - 1, False, True, False)


CONV_STEPS = 6


def shifted_views(zc, z, along_rows):
    p0, s0, n = 0, T_PROMPT, NT
    yield 0, zc[:, p0 + 1:s0], z[:, p0:s0 - 1]
    yield 2, zc[:, p0:s0 - 1], z[:, p0 + 1:s0]
    if along_rows:
        rows = lambda t: t[:, s0:n].rearrange("p (r w) -> p r w", w=GRID_W)
        yield 0, rows(zc)[:, :, 1:GRID_W], rows(z)[:, :, 0:GRID_W - 1]
        yield 2, rows(zc)[:, :, 0:GRID_W - 1], rows(z)[:, :, 1:GRID_W]
    else:
        yield 0, zc[:, s0 + GRID_W:n], z[:, s0:n - GRID_W]
        yield 2, zc[:, s0:n - GRID_W], z[:, s0 + GRID_W:n]


def gates(nc, io, h_hi, h_lo, z_hi, z_lo):
    with ExitStack() as ctx:
        sb = lambda n, shape: ctx.enter_context(nc.sbuf_tensor(n, shape, F32))
        sem = lambda n: nc.alloc_semaphore(n)
        ws = WeightStream(nc, ctx, "wg", io["w_gates"])
        ya_ps = ctx.enter_context(nc.psum_tensor("g_ya", [P, 2, 2, 512], F32))
        gate_ps = ctx.enter_context(nc.psum_tensor("g_ps", [P, 2, 2, 512], F32))
        sig, out_a = sb("g_sig", [P, 4, NT]), sb("g_a", [P, 2, NT])
        sig_done, prod_done, stored_a, stored_b = sem("g_sig_d"), sem("g_prod"), sem("g_sta"), sem("g_stb")
        R = 5
        N = KT // 2
        block = ctx.enter_context(nc.Block())

        @block.sync
        def _(sync):
            gemm_loop(ws, sync, R * N)

        @block.tensor
        def _(pe):
            def body(i, first):
                for s in range(2):
                    if not first:
                        pe.wait_ge(prod_done, 2 * i + s - 1)
                    ws.products(pe, R * i, s, ya_ps[:, s], z_hi, z_lo, 0, True, True)
                for n in range(4):
                    if n >= 2 or not first:
                        pe.wait_ge(sig_done, 4 * i + n - 1)
                    full_product(ws, pe, R * i + 1 + n, gate_ps[:, n % 2], h_hi, h_lo)
            body(0, True)
            with pe.Fori(1, N) as i:
                body(i, False)

        @block.scalar
        def _(act):
            def epilogue(i, n):
                if n == 0:
                    return
                act.wait_ge(ws.used, 2 * (R * i + n) + 2)
                act.activation(halves(sig[:, n - 1, :]), gate_ps[:, (n - 1) % 2, :, 0:HALF], ACT.Sigmoid
                               ).then_inc(sig_done, 1)
                if n in (2, 4):
                    s = n // 2 - 1
                    act.wait_ge(sig_done, 4 * i + n)
                    act.dma_start(row(io["gate_b"], 2 * i + s), sig[:, n - 1, :]).then_inc(stored_b, 16)
                    act.wait_ge(prod_done, 2 * i + s + 1)
                    act.dma_start(row(io["gated_a"], 2 * i + s), out_a[:, s, :]).then_inc(stored_a, 16)

            def body(i, first, last):
                if not first:
                    act.wait_ge(stored_b, 32 * i)
                    act.wait_ge(prod_done, 2 * i)
                for n in range(R):
                    if not (last and n == R - 1):
                        for slot in range(2):
                            ws.split_hi(act, R * i + n + 1, slot)
                    epilogue(i, n)
            for slot in range(2):
                ws.split_hi(act, 0, slot)
            body(0, True, False)
            with act.Fori(1, N - 1) as i:
                body(i, False, False)
            body(N - 1, False, True)
            act.wait_ge(stored_a, 32 * N)
            act.wait_ge(stored_b, 32 * N)

        @block.vector
        def _(dve):
            def body(i, first, last):
                if not first:
                    dve.wait_ge(stored_a, 32 * i)
                for n in range(R):
                    if not (last and n == R - 1):
                        for slot in range(2):
                            ws.split_lo(dve, R * i + n + 1, slot)
                    if n in (2, 4):
                        s = n // 2 - 1
                        dve.wait_ge(sig_done, 4 * i + 2 * s + 1)
                        dve.tensor_tensor(halves(out_a[:, s, :]), halves(sig[:, 2 * s, :]),
                                          ya_ps[:, s, :, 0:HALF], ALU.mult).then_inc(prod_done, 1)
            for slot in range(2):
                ws.split_lo(dve, 0, slot)
            body(0, True, False)
            with dve.Fori(1, N - 1) as i:
                body(i, False, False)
            body(N - 1, False, True)


def project_to_dram(nc, io, name, dram, count, out_dram, x_hi, x_lo, funcs=None):
    with ExitStack() as ctx:
        sem = lambda n: nc.alloc_semaphore(name + n)
        ws = WeightStream(nc, ctx, name + "_w", dram)
        ps = ctx.enter_context(nc.psum_tensor(name + "_ps", [P, 2, 2, 512], F32))
        out = ctx.enter_context(nc.sbuf_tensor(name + "_out", [P, 2, NT], F32))
        copied, stored = sem("_copied"), [sem(f"_stored{s}") for s in range(2)]
        N = count // 2
        block = ctx.enter_context(nc.Block())

        @block.sync
        def _(sync):
            gemm_loop(ws, sync, count)

        @block.tensor
        def _(pe):
            def body(i, first):
                for s in range(2):
                    if not first:
                        pe.wait_ge(copied, 2 * i + s - 1)
                    full_product(ws, pe, 2 * i + s, ps[:, s], x_hi, x_lo)
            body(0, True)
            with pe.Fori(1, N) as i:
                body(i, False)

        def act_body(act, i, first, last, func):
            for s in range(2):
                if not (last and s):
                    for slot in range(2):
                        ws.split_hi(act, 2 * i + s + 1, slot)
                act.wait_ge(ws.used, 2 * (2 * i + s) + 2)
                if not first:
                    act.wait_ge(stored[s], 16 * i)
                act.activation(halves(out[:, s, :]), ps[:, s, :, 0:HALF], func).then_inc(copied, 1)
                act.wait_ge(copied, 2 * i + s + 1)
                act.dma_start(row(out_dram, 2 * i + s), out[:, s, :]).then_inc(stored[s], 16)

        @block.scalar
        def _(act):
            for slot in range(2):
                ws.split_hi(act, 0, slot)
            if funcs:
                for i in range(N):
                    act_body(act, i, i == 0, i == N - 1, funcs[i])
            else:
                act_body(act, 0, True, False, ACT.Copy)
                with act.Fori(1, N - 1) as i:
                    act_body(act, i, False, False, ACT.Copy)
                act_body(act, N - 1, False, True, ACT.Copy)
            for s in range(2):
                act.wait_ge(stored[s], 16 * N)

        @block.vector
        def _(dve):
            for slot in range(2):
                ws.split_lo(dve, 0, slot)
            with dve.Fori(1, count) as r:
                for slot in range(2):
                    ws.split_lo(dve, r, slot)


def rwkv(nc, io):
    C = 64
    NC = NT // C
    LEVELS = 6
    NL = (LEVELS - 1) * NB
    STEPS_S = T_SAMPLE // C
    with ExitStack() as ctx:
        def sb(name, *shape, dt=F32):
            return ctx.enter_context(nc.sbuf_tensor("r_" + name, [P, *shape], dt))

        def sem(name):
            return nc.alloc_semaphore("r_" + name)

        masks = sb("masks", LEVELS + 1, 2, P)
        ident = sb("ident", P)
        causal = sb("causal", 2, 2, P)
        head_ones, keep, eps = sb("head_ones", P), sb("keep", NT), sb("eps", 3)
        par = sb("par", NJ, 10)
        low = sb("low", 6, NT)
        rkv, up, st = sb("rkv", 3, NT), sb("up", 6, P), sb("st", 2, 2, HEAD)
        kk, rk, q1 = sb("kk", NT), sb("rk", NT), sb("q1", NT)
        sg, aa, ps_, kd = sb("sg", 2, NT), sb("aa", 2, NT), sb("cum", NT), sb("kd", 2, NT)
        e_l, e_e, e_m = sb("e_l", NT), sb("e_e", NT), sb("e_m", NT)
        th = sb("th", 2, NC)
        t1, t2, t2b, o, cen = q1, e_l, e_e, e_m, kk
        b_t, k_t = sb("b_t", 2, 2, NT), sb("k_t", 2, 2, NT)
        a_t, r_t = sb("a_t", 2, 2, NT), sb("r_t", 2, 2, NT)
        e_h = sb("e_h", 2, 2, NC)
        gate, bonus = sb("gate", 2, NT), sb("bonus", 2, NT)
        v_tok, b_k_tok = sb("v_tok", NB, P), sb("bk_tok", NB, 4, P)
        ka, br, kr, m_t, x, x_t = (sb(n, NB, 4, P) for n in ("ka", "br", "kr", "m_t", "x", "x_t"))
        m_l, mx = sb("m_l", 2, 4, P), sb("mx", 2, 4, P)
        w_u, u = sb("w_u", 2, 4, HEAD), sb("u", NB, 4, HEAD)
        s_in = sb("s_in", STEPS_S + 1, 2, 2, HEAD)
        s_sum, s_out = sb("s_sum", 2, 2, HEAD), sb("s_out", 2, HEAD)
        aux = ctx.enter_context(nc.psum_tensor("r_aux", [P, 2, 512], F32))
        bank = ctx.enter_context(nc.psum_tensor("r_bank", [P, 6, 4, P], F32))

        const_loaded, par_done = sem("const"), sem("par")
        in_loaded = sem("in")
        aux_done = {n: sem("aux_" + n) for n in ("wf", "af", "wb", "ab", "gate", "ss", "bonus", "vtok", "mu", "var")}
        low_read = sem("low_read")
        kk_raw, kk_sq, kk_root, kk_inv, kk_done = sem("kk_raw"), sem("kk_sq"), sem("kk_root"), sem("kk_inv"), sem("kk")
        cum, centred, exps = sem("cum"), sem("centred"), sem("exps")
        kd_done, ops_done, rk_done, bonus_done = sem("kd"), sem("ops"), sem("rk"), sem("bonus")
        vtok_done, prod_out, prod_read, bktok_done, x_init = (
            sem("vtok"), sem("prod"), sem("prod_rd"), sem("bktok"), sem("x_init"))
        ml_done, t_out, t_read, d_out, x_add = sem("ml"), sem("t_out"), sem("t_rd"), sem("d_out"), sem("x_add")
        w_out, w_read, u_out, u_read, s_ps, s_step = (
            sem("w_out"), sem("w_rd"), sem("u_out"), sem("u_rd"), sem("s_ps"), sem("s_step"))
        o_out, o_read, cen_done, root2, norm_done, y_done = (
            sem("o_out"), sem("o_rd"), sem("cen"), sem("root2"), sem("normd"), sem("y"))
        y_stored, s_stored, s_final = sem("y_st"), sem("s_st"), sem("s_fin")
        block = ctx.enter_context(nc.Block())

        def chunk_of(d, s, lane):
            first_chunk, n = ((T_PROMPT // C, STEPS_S), (0, T_PROMPT // C))[lane]
            return first_chunk + (s if d == 0 else n - 1 - s)

        lanes = lambda s: (0, 1) if s < T_PROMPT // C else (0,)
        chunks = lambda t: t.rearrange("p (c t) -> p c t", c=NC)
        cols = lambda c: slice(c * P, (c + 1) * P)
        rows = lambda h: slice(h * HEAD, (h + 1) * HEAD)
        by_unit = lambda mask: mask[:, :, None, :].to_broadcast((P, 2, 2, P))
        param = lambda j, n: par[:, at(j), n:n + 1].rearrange("p a n -> p (a n)")
        STEPS = 16
        slot_of = {1 + 3 * k // 2: k for k in range(STEPS)}

        def prepare_pe(pe, k, j, jh, b, first):
            if k < 5:
                name = ("wf", "af", "wb", "ab", "gate")[k]
                if k == 0:
                    pe.wait_ge(in_loaded, 48 * j + 48)
                    if not first:
                        pe.wait_ge(vtok_done, j)
                else:
                    pe.wait_ge(low_read, 5 * j + k)
                for a in range(2):
                    col = slice(a * HALF, (a + 1) * HALF)
                    if k < 4:
                        n = (0, 2, 1, 3)[k]
                        last = pe.matmul(aux[:, a, 0:HALF], up[:, n, :], low[:, n, col], start=True, stop=True)
                    else:
                        for n in (4, 5):
                            last = pe.matmul(aux[:, a, 0:HALF], up[:, n, :], low[:, n, col],
                                             start=(n == 4), stop=(n == 5))
                last.then_inc(aux_done[name], 1)
            if k == 6:
                pe.wait_ge(low_read, 5 * j + 5)
                pe.wait_ge(kk_sq, j + 1)
                sum_heads(pe, t1).then_inc(aux_done["ss"], 1)
            if k == 15:
                pe.wait_ge(kk_root, j + 1)
                pe.wait_ge(rk_done, j + 1)
                sum_heads(pe, rk).then_inc(aux_done["bonus"], 1)

        def sum_heads(pe, src):
            for a in range(2):
                last = pe.matmul(aux[:, a, 0:HALF], head_ones[:], src[:, a * HALF:(a + 1) * HALF],
                                 start=True, stop=True)
            return last

        def prepare_act(act, k, j, jh, b, first):
            if k < 4:
                if k == 0 and not first:
                    act.wait_ge(rk_done, j)
                act.wait_ge(aux_done[("wf", "af", "wb", "ab")[k]], j + 1)
                dst = (sg, aa, sg, aa)[k][:, k // 2, :]
                act.activation(halves(dst), aux[:, :, 0:HALF], ACT.Sigmoid, bias=param(j, (0, 2, 1, 3)[k])
                               ).then_inc(low_read, 1)
            if k == 4:
                act.wait_ge(aux_done["gate"], j + 1)
                act.activation(halves(gate[:, b, :]), aux[:, :, 0:HALF], ACT.Copy).then_inc(low_read, 1)
            if k == 6:
                act.wait_ge(aux_done["ss"], j + 1)
                if not first:
                    act.wait_ge(ops_done, 2 * j)
                act.activation(halves(t2[:]), aux[:, :, 0:HALF], ACT.Sqrt, bias=eps[:, 2:3]).then_inc(kk_root, 1)
            if k in (8, 12):
                d = (k - 8) // 4
                act.wait_ge(centred, 6 * j + 3 * d + 3)
                if not (first and d == 0):
                    act.wait_ge(ops_done, 2 * j + d)
                fwd = ((e_l, ps_, -1), (e_e, q1, -1), (e_m, ps_, 1))
                bwd = ((e_l, q1, 1), (e_e, ps_, 1), (e_m, q1, -1))
                for dst, src, sign in (fwd, bwd)[d]:
                    act.activation(dst[:], src[:], ACT.Exp, scale=sign * DECAY_RATE).then_inc(exps, 1)
                act.activation(e_h[:, b, d, :], th[:, d, :], ACT.Exp, scale=-DECAY_RATE).then_inc(exps, 1)

        def prepare_dve(dve, k, j, jh, b, first):
            r, kx, v = (rkv[:, n, :] for n in range(3))
            if k == 5:
                dve.wait_ge(in_loaded, 48 * j + 48)
                if not isinstance(j, int) or j > 1:
                    dve.wait_ge(y_stored, 16 * (j - 1))
                dve.tensor_scalar(kk[:], kx, param(j, 4), None, ALU.mult).then_inc(kk_raw, 1)
                dve.tensor_scalar(rk[:], r, param(j, 7), None, ALU.mult).then_inc(kk_raw, 1)
                dve.wait_ge(kk_raw, 2 * j + 2)
                dve.tensor_tensor(t1[:], kk[:], kk[:], ALU.mult).then_inc(kk_sq, 1)
            if k == 6:
                dve.wait_ge(kk_root, j + 1)
                dve.reciprocal(t2[:], t2[:]).then_inc(kk_inv, 1)
                dve.wait_ge(kk_inv, j + 1)
                dve.tensor_tensor(kk[:], kk[:], t2[:], ALU.mult).then_inc(kk_done, 1)
            if k in (7, 11):
                d = (k - 7) // 4
                dve.wait_ge(low_read, 5 * j + 3)
                if not (first and d == 0):
                    dve.wait_ge(exps, 8 * j + 4 * d)
                dve.tensor_tensor_scan(ps_[:], keep[:], sg[:, d, :], 0.0, ALU.mult, ALU.add).then_inc(cum, 1)
                dve.wait_ge(cum, 2 * j + d + 1)
                dve.tensor_scalar(th[:, d, :, None], chunks(ps_[:])[:, :, C - 1:C], 0.5, None, ALU.mult
                                  ).then_inc(centred, 1)
                dve.wait_ge(centred, 6 * j + 3 * d + 1)
                dve.tensor_tensor(chunks(ps_[:]), chunks(ps_[:]), th[:, d, :, None].to_broadcast((P, NC, C)),
                                  ALU.subtract).then_inc(centred, 1)
                dve.wait_ge(centred, 6 * j + 3 * d + 2)
                dve.tensor_tensor(q1[:], ps_[:], sg[:, d, :], ALU.subtract).then_inc(centred, 1)
            if k in (8, 12):
                d = (k - 8) // 4
                dve.wait_ge(low_read, 5 * j + 4)
                dve.tensor_scalar(kd[:, d, :], aa[:, d, :], param(j, 5), param(j, 6), ALU.mult, ALU.add
                                  ).then_inc(kd_done, 1)
                dve.wait_ge(kk_done, j + 1)
                dve.tensor_tensor(aa[:, d, :], aa[:, d, :], kk[:], ALU.mult).then_inc(kd_done, 1)
                dve.wait_ge(kd_done, 6 * j + 3 * d + 1)
                dve.tensor_tensor(kd[:, d, :], kd[:, d, :], kx, ALU.mult).then_inc(kd_done, 1)
            if k in (9, 13):
                d = (k - 9) // 4
                dve.wait_ge(exps, 8 * j + 4 * d + 4)
                dve.wait_ge(kd_done, 6 * j + 3 * d + 3)
                dve.tensor_tensor(a_t[:, b, d, :], kk[:], e_e[:], ALU.mult)
                for h in range(2):
                    dve.scalar_tensor_tensor(b_t[rows(h), d, h, :], aa[rows(h), d, :], -1.0, e_m[rows(h), :],
                                             ALU.mult, ALU.mult)
            if k in (10, 14):
                d = (k - 10) // 4
                for h in range(2):
                    dve.tensor_tensor(k_t[rows(h), d, h, :], kd[rows(h), d, :], e_m[rows(h), :], ALU.mult)
                dve.tensor_tensor(r_t[:, b, d, :], r, e_l[:], ALU.mult).then_inc(ops_done, 1)
            if k == 15:
                dve.tensor_tensor(t1[:], kd[:, 0, :], kd[:, 1, :], ALU.add).then_inc(kd_sum, 1)
                dve.wait_ge(kd_sum, j + 1)
                dve.tensor_tensor(rk[:], rk[:], t1[:], ALU.mult).then_inc(rk_done, 1)
                dve.wait_ge(aux_done["bonus"], j + 1)
                dve.tensor_tensor(halves(bonus[:, b, :]), aux[:, :, 0:HALF], halves(v), ALU.mult
                                  ).then_inc(bonus_done, 1)

        kd_sum = sem("kd_sum")

        SSTEP = 1 + 2 * (STEPS_S - 1)
        s_count = lambda j, s: SSTEP * j + 1 + 2 * s

        KINDS = 6

        def chunk_pe(pe, j, b, first, last_pair, prep):
            for c in range(NB):
                if c == 0:
                    pe.wait_ge(bonus_done, j + 1)
                    if not first:
                        pe.wait_ge(root2, j)
                last = pe.transpose(aux[:, c // 4, (c % 4) * P:(c % 4 + 1) * P], rkv[:, 2, cols(c)],
                                    ident[:])
            last.then_inc(aux_done["vtok"], 1)
            if not first:
                pe.wait_ge(o_read, j)
                pe.wait_ge(s_step, SSTEP * j)
            at_, rt_ = a_t[:, b], r_t[:, b]
            for c in range(NB):
                of = lambda t, d, h: t[:, d, cols(c)] if t is at_ or t is rt_ else t[:, d, h, cols(c)]
                for n, (lhs, rhs) in enumerate(((k_t, at_), (b_t, rt_), (k_t, rt_), (b_t, at_), (at_, b_t))):
                    if c:
                        pe.wait_ge(prod_read, 5 * (NB * j + c - 1) + n + 1)
                    for q in range(4):
                        d, h = q // 2, q % 2
                        last = pe.matmul(bank[:, n, q, :], of(lhs, d, h), of(rhs, d, h), start=True, stop=True)
                    last.then_inc(prod_out, 1)
                if c:
                    pe.wait_ge(bktok_done, NB * j + c)
                for q in range(4):
                    for h in range(2):
                        src = (b_t, k_t)[q // 2]
                        last = pe.matmul(bank[:, 5, q, rows(h)], src[:, q % 2, h, cols(c)], ident[:, rows(h)],
                                         start=True, stop=True)
                last.then_inc(prod_out, 1)

            def first_product(n):
                c = n % NB
                pe.wait_ge(ml_done, NL * j + n + 1)
                if n < NB:
                    pe.wait_ge(x_init, 2 * (NB * j + c) + 2)
                    if n < 2:
                        pe.wait_ge(prod_read, 5 * (NB * j + NB))
                else:
                    pe.wait_ge(x_add, 2 * (NL * j + n - NB) + 2)
                if n >= 2:
                    pe.wait_ge(t_read, NL * j + n - 1)
                for q in range(4):
                    last = pe.matmul(bank[:, n % 2, q, :], m_l[:, n % 2, q, :], x[:, c, q, :],
                                     start=True, stop=True)
                last.then_inc(t_out, 1)

            def second_products(n):
                c = n % NB
                pe.wait_ge(t_read, NL * j + n + 1)
                if n < 2:
                    pe.wait_ge(bktok_done, NB * j + NB)
                else:
                    pe.wait_ge(x_add, 2 * (NL * j + n - 2) + 2)
                for q in range(4):
                    pe.matmul(bank[:, 2 + 2 * (n % 2), q, :], x_t[:, c, q, :], mx[:, n % 2, q, :],
                              start=True, stop=True)
                for q in range(4):
                    last = pe.matmul(bank[:, 3 + 2 * (n % 2), q, :], mx[:, n % 2, q, :], x_t[:, c, q, :],
                                     start=True, stop=True)
                last.then_inc(d_out, 1)

            first_product(0)
            for n in range(NL):
                if n + 1 < NL:
                    first_product(n + 1)
                second_products(n)
                prep(n)
            pe.wait_ge(vtok_done, j + 1)
            pe.wait_ge(x_add, 2 * NL * (j + 1))
            for s in range(STEPS_S):
                pe.wait_ge(s_step, s_count(j, s))
                if s:
                    pe.wait_ge(w_read, STEPS_S * j + s)
                for lane in lanes(s):
                    for q in range(4):
                        d, h = q // 2, q % 2
                        c = chunk_of(d, s, lane) // 2
                        out = bank[:, 0].rearrange("p l (q v) -> p (l q) v", v=HEAD)[:, 4 * lane + q, :]
                        enters = lane == 0 or s > 0
                        last = pe.matmul(out, ka[:, c, q, :], v_tok[:, c, rows(h)], start=True, stop=not enters)
                        if enters:
                            state = s_in[:, s if lane == 0 else STEPS_S, d, h, :]
                            last = pe.matmul(out, a_t[:, b, d, cols(c)], state, start=False, stop=True)
                last.then_inc(w_out, 1)
                pe.wait_ge(w_read, STEPS_S * j + s + 1)
                for lane in lanes(s):
                    for q in range(4):
                        c = chunk_of(q // 2, s, lane) // 2
                        out = bank[:, 1].rearrange("p l (q v) -> p (l q) v", v=HEAD)[:, 4 * lane + q, :]
                        last = pe.matmul(out, x_t[:, c, q, :], w_u[:, lane, q, :], start=True, stop=True)
                last.then_inc(u_out, 1)
                if s == STEPS_S - 1:
                    continue
                pe.wait_ge(const_loaded, 16 * 8)
                pe.wait_ge(u_read, STEPS_S * j + s + 1)
                for d in range(2):
                    for lane in lanes(s):
                        c = chunk_of(d, s, lane)
                        half = rows(c % 2)
                        for h in range(2):
                            out = bank[rows(h), (2, 5)[d], lane, 0:HEAD]
                            pe.matmul(out, b_k_tok[half, c // 2, d, rows(h)], u[half, c // 2, 2 * d + h, :],
                                      start=True, stop=False)
                            last = pe.matmul(out, b_k_tok[half, c // 2, 2 + d, rows(h)], v_tok[half, c // 2, rows(h)],
                                             start=False, stop=True)
                    last.then_inc(s_ps, 1)
            pe.wait_ge(u_read, STEPS_S * (j + 1))
            for c in range(NB):
                for h in range(2):
                    out = bank[rows(h), 3 + c // 4, c % 4, :]
                    for d in range(2):
                        q = 2 * d + h
                        pe.matmul(out, v_tok[:, c, rows(h)], kr[:, c, q, :], start=(d == 0), stop=False)
                        for half in range(2):
                            chunk = 2 * c + half
                            lane = 0 if c else 1
                            s = [s for s in range(STEPS_S) if chunk_of(d, s, lane) == chunk][0]
                            if lane == 1 and s == 0:
                                continue
                            state = s_in[:, s if lane == 0 else STEPS_S, d, h, :]
                            pe.matmul(out[:, half * C:(half + 1) * C], state,
                                      r_t[:, b, d, chunk * C:(chunk + 1) * C], start=False, stop=False)
                        last = pe.matmul(out, u[:, c, q, :], br[:, c, q, :], start=False, stop=(d == 1))
            last.then_inc(o_out, 1)
            pe.wait_ge(o_read, j + 1)
            if not last_pair:
                pe.wait_ge(bonus_done, j + 2)
            sum_heads(pe, o).then_inc(aux_done["mu"], 1)
            pe.wait_ge(cen_done, 2 * j + 2)
            sum_heads(pe, o).then_inc(aux_done["var"], 1)


        def chunk_act(act, j, b, first, last_pair, prep):
            act.wait_ge(aux_done["vtok"], j + 1)
            act.activation(v_tok[:, 0:4, :], aux[:, 0, :].rearrange("p (c t) -> p c t", c=4), ACT.Copy)
            act.activation(v_tok[:, 4, :], aux[:, 1, 0:P], ACT.Copy).then_inc(vtok_done, 1)
            for c in range(NB):
                act.wait_ge(prod_out, KINDS * (NB * j + c + 1))
                act.activation(b_k_tok[:, c], bank[:, 5], ACT.Copy).then_inc(bktok_done, 1)
            for n in range(NL):
                act.wait_ge(t_out, NL * j + n + 1)
                if n >= 2:
                    act.wait_ge(d_out, NL * j + n - 1)
                act.activation(mx[:, n % 2], bank[:, n % 2], ACT.Copy).then_inc(t_read, 1)
                prep(n)
            for s in range(STEPS_S):
                n = len(lanes(s))
                act.wait_ge(w_out, STEPS_S * j + s + 1)
                act.activation(w_u[:, 0:n].rearrange("p l q v -> p (l q v)"),
                               bank[:, 0].rearrange("p q t -> p (q t)")[:, 0:4 * HEAD * n], ACT.Copy
                               ).then_inc(w_read, 1)
                act.wait_ge(u_out, STEPS_S * j + s + 1)
                for lane in lanes(s):
                    for d in range(2):
                        c = chunk_of(d, s, lane)
                        half = rows(c % 2)
                        src = bank[half, 1].rearrange("p l (q v) -> p (l q) v", v=HEAD)
                        at_q = 4 * lane + 2 * d
                        last = act.activation(u[half, c // 2, 2 * d:2 * d + 2, :], src[:, at_q:at_q + 2, :], ACT.Copy)
                last.then_inc(u_read, 1)
            act.wait_ge(o_out, j + 1)
            if not first:
                act.wait_ge(cen_done, 2 * j)
            act.activation(o[:, 0:4 * P], bank[:, 3].rearrange("p c t -> p (c t)"), ACT.Copy)
            act.activation(o[:, 4 * P:NT], bank[:, 4, 0, :], ACT.Copy).then_inc(o_read, 1)
            act.wait_ge(aux_done["var"], j + 1)
            act.activation(halves(t2b[:]), aux[:, :, 0:HALF], ACT.Sqrt, scale=1.0 / HEAD, bias=eps[:, 1:2]
                           ).then_inc(root2, 1)

        def chunk_pool(pool, j, b, first):
            level = lambda l: by_unit(masks[:, l])
            units4 = lambda t: t.rearrange("p (d h) n -> p d h n", d=2)
            for c in range(NB):
                pool.wait_ge(prod_read, 5 * (NB * j + c + 1))
                pool.tensor_tensor(x[:, c], x[:, c], ident[:, None, :].to_broadcast((P, 4, P)), ALU.add).then_inc(x_init, 1)
                pool.tensor_tensor(units4(x_t[:, c]), units4(m_t[:, c]), level(0), ALU.mult).then_inc(xt_half, 1)
                pool.wait_ge(xt_half, NB * j + c + 1)
                pool.tensor_tensor(x_t[:, c], x_t[:, c], ident[:, None, :].to_broadcast((P, 4, P)), ALU.add).then_inc(x_init, 1)
                if c < 2:
                    first_masks(pool, j, c, first)
            for n in range(2, NL):
                pool.wait_ge(t_out, NL * j + n - 1)
                pool.tensor_tensor(units4(m_l[:, n % 2]), units4(m_t[:, n % NB]), level(1 + n // NB), ALU.mult
                                   ).then_inc(ml_done, 1)

        def first_masks(pool, j, c, first):
            units4 = lambda t: t.rearrange("p (d h) n -> p d h n", d=2)
            pool.tensor_tensor(units4(m_l[:, c]), units4(m_t[:, c]), by_unit(masks[:, 1]), ALU.mult
                               ).then_inc(ml_done, 1)

        def chunk_dve(dve, j, b, first, last_pair, prep):
            if first:
                dve.memset(s_in[:], 0.0).then_inc(zeroed, 1)
                dve.wait_ge(zeroed, 3)
            units4 = lambda t: t.rearrange("p (d h) n -> p d h n", d=2)
            for c in range(NB):
                for n, (dst, mask) in enumerate(((ka, causal[:, 0]), (br, causal[:, 1]), (kr, causal[:, 1]),
                                                 (m_t, causal[:, 0]), (x, masks[:, LEVELS]))):
                    dve.wait_ge(prod_out, KINDS * (NB * j + c) + n + 1)
                    dve.tensor_tensor(units4(dst[:, c]), units4(bank[:, n]), by_unit(mask), ALU.mult
                                      ).then_inc(prod_read, 1)
            for n in range(NL):
                c = n % NB
                dve.wait_ge(d_out, NL * j + n + 1)
                for t, k in ((x, 2), (x_t, 3)):
                    dve.tensor_tensor(t[:, c], t[:, c], bank[:, k + 2 * (n % 2)], ALU.add).then_inc(x_add, 1)
                prep(n)
            for d in range(2):
                c = chunk_of(d, 0, 0)
                for h in range(2):
                    last = dve.tensor_scalar(s_in[rows(h), 0, d, h, :], st[rows(h), b, d, :],
                                             e_h[rows(h), b, d, c:c + 1], None, ALU.mult)
            last.then_inc(s_step, 1)
            if not first:
                dve.wait_ge(s_stored, 16 * j)
            for s in range(STEPS_S - 1):
                dve.wait_ge(s_ps, 2 * (STEPS_S - 1) * j + 2 * s + 2)
                for lane in lanes(s):
                    for d in range(2):
                        for h in range(2):
                            src, dst = bank[rows(h), (2, 5)[d], lane, 0:HEAD], s_sum[rows(h), lane, d, :]
                            if lane == 1 and s == 0:
                                last = dve.tensor_copy(dst, src)
                            else:
                                state = s_in[rows(h), s if lane == 0 else STEPS_S, d, h, :]
                                last = dve.tensor_tensor(dst, src, state, ALU.add)
                last.then_inc(s_step, 1)
                dve.wait_ge(s_step, s_count(j, s) + 1)
                for lane in lanes(s):
                    for d in range(2):
                        c = chunk_of(d, s, lane)
                        if lane == 1 and s == 1:
                            last = dve.tensor_scalar(s_out[:, d, :], s_sum[:, 1, d, :], e_h[:, b, d, c:c + 1], None,
                                                     ALU.mult)
                            continue
                        c2 = chunk_of(d, s + 1, lane)
                        for h in range(2):
                            dst = s_in[rows(h), s + 1 if lane == 0 else STEPS_S, d, h, :]
                            last = dve.tensor_scalar(dst, s_sum[rows(h), lane, d, :], e_h[rows(h), b, d, c:c + 1],
                                                     e_h[rows(h), b, d, c2:c2 + 1], ALU.mult, ALU.mult)
                last.then_inc(s_step, 1)
            dve.wait_ge(aux_done["mu"], j + 1)
            if last_pair:
                dve.wait_ge(y_stored, 16 * j)
            dve.scalar_tensor_tensor(halves(cen[:]), aux[:, :, 0:HALF], -1.0 / HEAD, halves(o[:]), ALU.mult, ALU.add
                                     ).then_inc(cen_done, 1)
            dve.wait_ge(cen_done, 2 * j + 1)
            dve.tensor_tensor(o[:], cen[:], cen[:], ALU.mult).then_inc(cen_done, 1)
            dve.wait_ge(root2, j + 1)
            dve.reciprocal(t2b[:], t2b[:]).then_inc(norm_done, 1)
            dve.wait_ge(norm_done, 4 * j + 1)
            dve.tensor_tensor(cen[:], cen[:], t2b[:], ALU.mult).then_inc(norm_done, 1)
            dve.wait_ge(norm_done, 4 * j + 2)
            dve.tensor_scalar(cen[:], cen[:], param(j, 8), param(j, 9), ALU.mult, ALU.add).then_inc(norm_done, 1)
            dve.wait_ge(norm_done, 4 * j + 3)
            dve.tensor_tensor(cen[:], cen[:], bonus[:, b, :], ALU.add).then_inc(norm_done, 1)
            dve.wait_ge(norm_done, 4 * j + 4)
            dve.tensor_tensor(cen[:], cen[:], gate[:, b, :], ALU.mult).then_inc(y_done, 1)

        xt_half, zeroed = sem("xt_half"), sem("zeroed")

        def run(eng, prepare, chunk):
            for k in range(STEPS):
                prepare(eng, k, 0, 0, 0, True)

            def body(j, jh, b, first, last):
                def prep(n):
                    if not last and n in slot_of:
                        prepare(eng, slot_of[n], j + 1, jh + b, 1 - b, False)
                chunk(eng, j, b, first, last, prep)
            body(0, 0, 0, True, False)
            with eng.Fori(0, (NJ - 2) // 2) as i:
                body(2 * i + 1, i, 1, False, False)
                body(2 * i + 2, i + 1, 0, False, False)
            body(NJ - 1, (NJ - 1) // 2, 1, False, True)

        @block.tensor
        def _(pe):
            pe.wait_ge(const_loaded, 16 * 8)
            run(pe, prepare_pe, chunk_pe)

        @block.scalar
        def _(act):
            act.wait_ge(const_loaded, 16 * 8)
            run(act, prepare_act, chunk_act)

        @block.vector
        def _(dve):
            dve.wait_ge(const_loaded, 16 * 8)
            dve.tensor_scalar(par[:, :, 6:7], par[:, :, 5:6], -1.0, 1.0, ALU.mult, ALU.add).then_inc(par_done, 1)
            for t in (b_t, k_t):
                dve.memset(t[:], 0.0).then_inc(zeroed, 1)
            dve.wait_ge(zeroed, 2)
            dve.wait_ge(par_done, 1)
            run(dve, prepare_dve, chunk_dve)

        @block.gpsimd
        def _(pool):
            pool.wait_ge(const_loaded, 16 * 8)
            run(pool, lambda *a: None, lambda eng, j, b, first, last, prep: chunk_pool(eng, j, b, first))

        @block.sync
        def _(sync):
            def load(j, b):
                sync.dma_start(rkv[:], row(io["rkv"].rearrange("(j n) p t -> j p n t", n=3), j)
                               ).then_inc(in_loaded, 16)
                sync.dma_start(up[:], row(io["w_low"], j)).then_inc(in_loaded, 16)
                sync.dma_start(st[:, b], row(io["state"], j)).then_inc(in_loaded, 16)

            for dst, src in ((masks, "r_masks"), (ident, "ident"), (causal, "r_causal"), (head_ones, "r_head_ones"),
                             (keep, "r_keep"), (eps, "eps"), (par, "r_par")):
                sync.dma_start(dst[:], io[src]).then_inc(const_loaded, 16)
            sync.dma_start(low[:], io["lora"].rearrange("n p t -> p n t")).then_inc(const_loaded, 16)
            load(0, 0)

            def body(j, b, last):
                if not last:
                    sync.wait_ge(aux_done["vtok"], j + 1)
                    load(j + 1, 1 - b)
                sync.wait_ge(s_step, s_count(j, 2))
                sync.dma_start(row(io["new_state"], j), s_out[:]).then_inc(s_stored, 16)
                sync.wait_ge(y_done, j + 1)
                sync.dma_start(row(io["y_b"], j), cen[:]).then_inc(y_stored, 16)
            body(0, 0, False)
            with sync.Fori(0, (NJ - 2) // 2) as i:
                body(2 * i + 1, 1, False)
                body(2 * i + 2, 0, False)
            body(NJ - 1, 1, True)
            sync.wait_ge(s_stored, 16 * NJ)
            sync.wait_ge(y_stored, 16 * NJ)


def split_y(nc, io, y_hi, y_lo):
    with ExitStack() as ctx:
        raw = ctx.enter_context(nc.sbuf_tensor("y_raw", [P, 4, NT], F32))
        loaded = [nc.alloc_semaphore(f"y_loaded{s}") for s in range(4)]
        hi_done, lo_done = nc.alloc_semaphore("y_hi_done"), nc.alloc_semaphore("y_lo_done")
        block = ctx.enter_context(nc.Block())

        @block.sync
        def _(sync):
            for j in range(NJ):
                if j >= 4:
                    sync.wait_ge(lo_done, j - 3)
                sync.dma_start(raw[:, j % 4, :], io["y_b"][j]).then_inc(loaded[j % 4], 16)

        @block.scalar
        def _(act):
            for j in range(NJ):
                act.wait_ge(loaded[j % 4], 16 * (j // 4 + 1))
                act.activation(y_hi[:, j, :], raw[:, j % 4, :], ACT.Copy).then_inc(hi_done, 1)

        @block.vector
        def _(dve):
            for j in range(NJ):
                dve.wait_ge(hi_done, j + 1)
                dve.tensor_tensor(y_lo[:, j, :], raw[:, j % 4, :], y_hi[:, j, :].bitcast(F32), ALU.subtract
                                  ).then_inc(lo_done, 1)


def merge(nc, io, y_hi, y_lo, m_hi, m_lo):
    with ExitStack() as ctx:
        sb = lambda n: ctx.enter_context(nc.sbuf_tensor("mg_" + n, [P, 2, NT], F32))
        sem = lambda n: nc.alloc_semaphore("mg_" + n)
        ws = WeightStream(nc, ctx, "wo", io["w_o"])
        ps = ctx.enter_context(nc.psum_tensor("mg_ps", [P, 2, 2, 512], F32))
        gated_a, gate_b = sb("a"), sb("b")
        loaded, gated, summed, hi_done, lo_done = ([sem("l0"), sem("l1")], sem("gated"), sem("sum"), sem("hi"), sem("lo"))
        N = KT // 2
        block = ctx.enter_context(nc.Block())

        @block.sync
        def _(sync):
            def body(i, first):
                for s in range(2):
                    for slot in range(2):
                        ws.load(sync, 2 * i + s, slot)
                    if not first:
                        sync.wait_ge(lo_done, 2 * i + s - 1)
                    sync.dma_start(gated_a[:, s, :], row(io["gated_a"], 2 * i + s)).then_inc(loaded[s], 16)
                    sync.dma_start(gate_b[:, s, :], row(io["gate_b"], 2 * i + s)).then_inc(loaded[s], 16)
            body(0, True)
            with sync.Fori(1, N) as i:
                body(i, False)

        @block.tensor
        def _(pe):
            def body(i, first):
                for s in range(2):
                    if not first:
                        pe.wait_ge(gated, 2 * i + s - 1)
                    full_product(ws, pe, 2 * i + s, ps[:, s], y_hi, y_lo)
            body(0, True)
            with pe.Fori(1, N) as i:
                body(i, False)

        @block.scalar
        def _(act):
            def body(i, last):
                for s in range(2):
                    if not (last and s):
                        for slot in range(2):
                            ws.split_hi(act, 2 * i + s + 1, slot)
                    act.wait_ge(summed, 2 * i + s + 1)
                    act.activation(m_hi[:, at(2 * i + s), :], gate_b[:, s:s + 1, :], ACT.Copy).then_inc(hi_done, 1)
            for slot in range(2):
                ws.split_hi(act, 0, slot)
            with act.Fori(0, N - 1) as i:
                body(i, False)
            body(N - 1, True)

        @block.vector
        def _(dve):
            def body(i, last):
                for s in range(2):
                    if not (last and s):
                        for slot in range(2):
                            ws.split_lo(dve, 2 * i + s + 1, slot)
                    dve.wait_ge(loaded[s], 32 * i + 32)
                    dve.wait_ge(ws.used, 2 * (2 * i + s) + 2)
                    dve.tensor_tensor(halves(gate_b[:, s, :]), halves(gate_b[:, s, :]), ps[:, s, :, 0:HALF],
                                      ALU.mult).then_inc(gated, 1)
                    dve.wait_ge(gated, 2 * i + s + 1)
                    dve.tensor_tensor(gate_b[:, s, :], gate_b[:, s, :], gated_a[:, s, :], ALU.add
                                      ).then_inc(summed, 1)
                    dve.wait_ge(hi_done, 2 * i + s + 1)
                    dve.tensor_tensor(m_lo[:, at(2 * i + s), :], gate_b[:, s:s + 1, :],
                                      m_hi[:, at(2 * i + s), :].bitcast(F32), ALU.subtract).then_inc(lo_done, 1)
            for slot in range(2):
                ws.split_lo(dve, 0, slot)
            with dve.Fori(0, N - 1) as i:
                body(i, False)
            body(N - 1, True)


def add_gated(dve, x, ps, gate):
    for (g, bank, t0, t1) in ((0, 0, 0, T_PROMPT), (1, 0, T_PROMPT, HALF), (1, 1, HALF, NT)):
        last = dve.scalar_tensor_tensor(x[:, t0:t1], ps[:, bank, t0 - bank * HALF:t1 - bank * HALF], gate(g),
                                        x[:, t0:t1], ALU.mult, ALU.add)
    return last


def mix(nc, io, m_hi, m_lo, gate1):
    with ExitStack() as ctx:
        sem = lambda n: nc.alloc_semaphore("mx_" + n)
        ws = WeightStream(nc, ctx, "wm", io["w_mix"])
        ps = ctx.enter_context(nc.psum_tensor("mx_ps", [P, 2, 2, 512], F32))
        x = ctx.enter_context(nc.sbuf_tensor("mx_x", [P, 2, NT], F32))
        loaded, added, stored = [sem("l0"), sem("l1")], sem("added"), [sem("st0"), sem("st1")]
        N = KT // 2
        block = ctx.enter_context(nc.Block())

        @block.sync
        def _(sync):
            def body(i, first):
                for s in range(2):
                    for slot in range(2):
                        ws.load(sync, 2 * i + s, slot)
                    if not first:
                        sync.wait_ge(stored[s], 16 * i)
                    sync.dma_start(x[:, s, :], row(io["x"], 2 * i + s)).then_inc(loaded[s], 16)
            body(0, True)
            with sync.Fori(1, N) as i:
                body(i, False)

        @block.tensor
        def _(pe):
            def body(i, first):
                for s in range(2):
                    if not first:
                        pe.wait_ge(added, 2 * i + s - 1)
                    full_product(ws, pe, 2 * i + s, ps[:, s], m_hi, m_lo)
            body(0, True)
            with pe.Fori(1, N) as i:
                body(i, False)

        @block.scalar
        def _(act):
            def body(i, last):
                for s in range(2):
                    if not (last and s):
                        for slot in range(2):
                            ws.split_hi(act, 2 * i + s + 1, slot)
                    act.wait_ge(added, 2 * i + s + 1)
                    act.dma_start(row(io["x1"], 2 * i + s), x[:, s, :]).then_inc(stored[s], 16)
            for slot in range(2):
                ws.split_hi(act, 0, slot)
            with act.Fori(0, N - 1) as i:
                body(i, False)
            body(N - 1, True)
            for s in range(2):
                act.wait_ge(stored[s], 16 * N)

        @block.vector
        def _(dve):
            def body(i, last):
                for s in range(2):
                    if not (last and s):
                        for slot in range(2):
                            ws.split_lo(dve, 2 * i + s + 1, slot)
                    dve.wait_ge(loaded[s], 16 * i + 16)
                    dve.wait_ge(ws.used, 2 * (2 * i + s) + 2)
                    gate = lambda g: gate1[:, at(2 * i + s), g:g + 1].rearrange("p a n -> p (a n)")
                    add_gated(dve, x[:, s, :], ps[:, s], gate).then_inc(added, 1)
            for slot in range(2):
                ws.split_lo(dve, 0, slot)
            with dve.Fori(0, N - 1) as i:
                body(i, False)
            body(N - 1, True)


def top_experts(nc, io, h_hi, h_lo, picks):
    H = PEER_HEADS
    LOWEST = -3.4e38
    with ExitStack() as ctx:
        sb = lambda n, *shape, dt=F32: ctx.enter_context(nc.sbuf_tensor("t_" + n, [P, *shape], dt))
        sem = lambda n: nc.alloc_semaphore("t_" + n)
        ws = WeightStream(nc, ctx, "wq", io["w_q"])
        keys, iota = sb("keys", 2 * H, N_KEYS), sb("iota", TOPK)
        q, scores, rest = sb("q", 2, NT), sb("scores", 2, NB, N_KEYS), sb("rest", NB, N_KEYS)
        val, idx, idx_f = sb("val", 2, NB, TOPK), sb("idx", 2, NB, TOPK, dt=U32), sb("idx_f", 2, NB, TOPK)
        cand, cand_rest = sb("cand", NB, TOPK * TOPK), sb("cand_rest", NB, TOPK * TOPK)
        top, pos = sb("top", NB, TOPK), sb("pos", NB, TOPK, dt=U32)
        ab, ab_f = sb("ab", 2, NB, TOPK, dt=U32), sb("ab_f", 2, NB, TOPK)
        chosen = sb("chosen", 2, NB * TOPK, TOPK)
        carrier = sb("carrier", TOPK)
        res, total = sb("res", 3, NB, TOPK), sb("total", NB)
        q_ps = ctx.enter_context(nc.psum_tensor("t_q_ps", [P, 2, 2, 512], F32))
        s_ps = ctx.enter_context(nc.psum_tensor("t_s_ps", [P, 2, 1024], F32))
        const_loaded, q_copied, scored, s_copied, ranked = (
            sem("const"), sem("q_copied"), sem("scored"), sem("s_copied"), sem("ranked"))
        step, shifted, exp_done = sem("step"), sem("shifted"), sem("exp")
        block = ctx.enter_context(nc.Block())

        @block.sync
        def _(sync):
            sync.dma_start(keys[:], io["sub_keys"]).then_inc(const_loaded, 16)
            sync.dma_start(iota[:], io["iota"][:, 0:TOPK]).then_inc(const_loaded, 16)
            gemm_loop(ws, sync, 2 * H)

        @block.tensor
        def _(pe):
            def body(i, first):
                for half in range(2):
                    r = 2 * i + half
                    if not first:
                        pe.wait_ge(q_copied, r - 1)
                    full_product(ws, pe, r, q_ps[:, half], h_hi, h_lo)
                    pe.wait_ge(q_copied, r + 1)
                    if not first:
                        pe.wait_ge(s_copied, r - 1)
                    for b in range(NB):
                        last = pe.matmul(s_ps[:, half, b * P:(b + 1) * P], q[:, half, b * P:(b + 1) * P],
                                         keys[:, at(r), :], start=True, stop=True)
                    last.then_inc(scored, 1)
            pe.wait_ge(const_loaded, 32)
            body(0, True)
            with pe.Fori(1, H) as i:
                body(i, False)

        @block.scalar
        def _(act):
            def body(i, first, last):
                for half in range(2):
                    r = 2 * i + half
                    if not (last and half):
                        for slot in range(2):
                            ws.split_hi(act, r + 1, slot)
                    act.wait_ge(ws.used, 2 * r + 2)
                    if not first:
                        act.wait_ge(scored, r - 1)
                    act.activation(halves(q[:, half, :]), q_ps[:, half, :, 0:HALF], ACT.Copy).then_inc(q_copied, 1)
                    act.wait_ge(scored, r + 1)
                    if not first:
                        act.wait_ge(ranked, r - 1)
                    act.activation(scores[:, half], s_ps[:, half, 0:NT].rearrange("p (b t) -> p b t", b=NB), ACT.Copy
                                   ).then_inc(s_copied, 1)
                act.wait_ge(shifted, i + 1)
                act.activation(res[:, 2], top[:], ACT.Exp).then_inc(exp_done, 1)
            for slot in range(2):
                ws.split_hi(act, 0, slot)
            body(0, True, False)
            with act.Fori(1, H - 1) as i:
                body(i, False, False)
            body(H - 1, False, True)

        @block.gpsimd
        def _(pool):
            for slot in range(2):
                ws.split_lo(pool, 0, slot)
            with pool.Fori(1, 2 * H) as r:
                for slot in range(2):
                    ws.split_lo(pool, r, slot)

        @block.vector
        def _(dve):
            STEPS = 20
            def body(i):
                done, used = [0], [0]

                def wait_apart(semaphore, value):
                    dve.wait_ge(semaphore, value)
                    dve.tensor_copy(carrier[:, used[0]:used[0] + 1], iota[:, 0:1])
                    used[0] += 1

                def after_steps():
                    wait_apart(step, STEPS * i + done[0])

                def finish(instruction):
                    done[0] += 1
                    instruction.then_inc(step, 1)

                def rank(v, n, src, left):
                    for b in range(NB):
                        last = dve.max(v[:, b, 0:8], src[:, b, :])
                    finish(last)
                    after_steps()
                    for b in range(NB):
                        dve.max_index(n[:, b, 0:8], v[:, b, 0:8], src[:, b, :])
                    for b in range(NB):
                        last = dve.match_replace(left[:, b, :], v[:, b, 0:8], src[:, b, :], LOWEST)
                    finish(last)
                    after_steps()
                    for b in range(NB):
                        last = dve.max(v[:, b, 8:16], left[:, b, :])
                    finish(last)
                    after_steps()
                    for b in range(NB):
                        last = dve.max_index(n[:, b, 8:16], v[:, b, 8:16], left[:, b, :])
                    return last

                for half in range(2):
                    wait_apart(s_copied, 2 * i + half + 1)
                    rank(val[:, half], idx[:, half], scores[:, half], rest).then_inc(ranked, 1)
                dve.wait_ge(ranked, 2 * i + 2)
                grid = (P, NB, TOPK, TOPK)
                pairs = lambda t: t.rearrange("p b (x y) -> p b x y", x=TOPK)
                finish(dve.tensor_tensor(pairs(cand[:]), val[:, 0, :, :, None].to_broadcast(grid),
                                         val[:, 1, :, None, :].to_broadcast(grid), ALU.add))
                after_steps()
                finish(rank(top, pos, cand, cand_rest))
                dve.wait_ge(step, STEPS * i + done[0])
                dve.tensor_scalar(ab[:, 0], pos[:], 4, None, ALU.logical_shift_right)
                finish(dve.tensor_scalar(ab[:, 1], pos[:], TOPK - 1, None, ALU.bitwise_and))
                finish(dve.tensor_tensor(cand[:, :, 0:TOPK], top[:], top[:, :, 0:1].to_broadcast((P, NB, TOPK)),
                                         ALU.subtract))
                dve.tensor_copy(idx_f[:], idx[:])
                dve.wait_ge(step, STEPS * i + done[0])
                dve.tensor_copy(top[:], cand[:, :, 0:TOPK]).then_inc(shifted, 1)
                finish(dve.tensor_copy(ab_f[:], ab[:]))
                dve.wait_ge(step, STEPS * i + done[0])
                flat = (P, NB * TOPK, TOPK)
                for n in range(2):
                    last = dve.tensor_tensor(chosen[:, n], iota[:, None, :].to_broadcast(flat),
                                             ab_f[:, n].rearrange("p b k -> p (b k)")[:, :, None].to_broadcast(flat),
                                             ALU.is_equal)
                finish(last)
                dve.wait_ge(step, STEPS * i + done[0])
                for n in range(2):
                    view = chosen[:, n].rearrange("p (b k) m -> p b k m", b=NB)
                    last = dve.tensor_tensor(view, view, idx_f[:, n, :, None, :].to_broadcast(grid), ALU.mult)
                finish(last)
                dve.wait_ge(step, STEPS * i + done[0])
                dve.tensor_reduce(res[:, 0:2].rearrange("p n b k -> p (n b k)"),
                                  chosen[:].rearrange("p n s m -> p (n s) m"), AX.X, ALU.add)
                dve.wait_ge(exp_done, i + 1)
                finish(dve.tensor_reduce(total[:], res[:, 2], AX.X, ALU.add))
                dve.wait_ge(step, STEPS * i + done[0])
                finish(dve.reciprocal(total[:], total[:]))
                dve.wait_ge(step, STEPS * i + done[0])
                finish(dve.tensor_tensor(res[:, 2], res[:, 2], total[:, :, None].to_broadcast((P, NB, TOPK)), ALU.mult))
                dve.wait_ge(step, STEPS * i + done[0])
                finish(dve.tensor_copy(picks[:, :, at(i), :], res[:].rearrange("p n b k -> p (n b) k")[:, :, None, :]))
                assert done[0] == STEPS, done
            dve.wait_ge(const_loaded, 32)
            with dve.Fori(0, H) as i:
                body(i)


def gate_matrix(nc, io, picks):
    SET = 4
    SETS = 4
    HB = P // 2
    BODIES = HB // (SET * SETS)
    with ExitStack() as ctx:
        sb = lambda n, *shape: ctx.enter_context(nc.sbuf_tensor("gm_" + n, [P, *shape], F32))
        sem = lambda n: nc.alloc_semaphore("gm_" + n)
        iota, ident = sb("iota", P), sb("ident", P)
        picks_t = sb("picks_t", 3, NT)
        hot1, hot2 = sb("hot1", SETS, SET, P), sb("hot2", SETS, SET, P)
        dense = sb("dense", 2, N_KEYS, HB)
        ps = ctx.enter_context(nc.psum_tensor("gm_ps", [P, SETS, SET, P], F32))
        t_ps = ctx.enter_context(nc.psum_tensor("gm_t_ps", [P, 4, 4, P], F32))
        const_loaded, turned, turned_out = sem("const"), sem("turned"), sem("turned_out")
        hot_done, dense_done, copied = sem("hot"), sem("dense"), sem("copied")
        stored = [sem("st0"), sem("st1")]
        block = ctx.enter_context(nc.Block())

        def over_sets(eng, body):
            def part(blk, half, k0):
                with eng.Fori(k0, BODIES) as k:
                    for s in range(SETS):
                        t = SET * SETS * k + SET * s
                        body(SETS * BODIES * (2 * blk + half) + SETS * k + s, s, P * blk + HB * half + t, half, t, False)

            def whole(blk, half, first, begin, end):
                begin(blk, half, first)
                if first and half == 0:
                    for s in range(SETS):
                        body(s, s, SET * s, 0, SET * s, True)
                    part(0, 0, 1)
                else:
                    part(blk, half, 0)
                end(blk, half)
            return whole

        def run(eng, body, begin=lambda *a: None, end=lambda *a: None):
            whole = over_sets(eng, body)
            for half in range(2):
                whole(0, half, True, begin, end)
            with eng.Fori(1, NB) as blk:
                for half in range(2):
                    whole(blk, half, False, begin, end)

        @block.sync
        def _(sync):
            sync.dma_start(iota[:], io["iota"]).then_inc(const_loaded, 16)
            sync.dma_start(ident[:], io["ident"]).then_inc(const_loaded, 16)

            def store(blk, half):
                sync.wait_ge(copied, SETS * BODIES * (2 * blk + half + 1))
                sync.dma_start(row(io["peer_gates"], 2 * blk + half), dense[:, half]).then_inc(stored[half], 16)
            for half in range(2):
                store(0, half)
            with sync.Fori(1, NB) as blk:
                for half in range(2):
                    store(blk, half)
            for half in range(2):
                sync.wait_ge(stored[half], 16 * NB)

        @block.vector
        def _(dve):
            def body(q, s, t0, half, t, first):
                if not first:
                    dve.wait_ge(dense_done, q - SETS + 1)
                index = picks_t[:, 0, t0:t0 + SET] if isinstance(t0, int) else picks_t[:, 0, bass.ds(t0, SET)]
                shape = (P, SET, P)
                dve.tensor_tensor(hot1[:, s], iota[:, None, :].to_broadcast(shape),
                                  index[:, :, None].to_broadcast(shape), ALU.is_equal)
                for n in range(SET):
                    col = lambda m: picks_t[:, m, t0 + n:t0 + n + 1] if isinstance(t0, int) else picks_t[:, m, bass.ds(t0 + n, 1)]
                    last = dve.tensor_scalar(hot2[:, s, n, :], iota[:], col(1), col(2), ALU.is_equal, ALU.mult)
                last.then_inc(hot_done, 1)
            dve.wait_ge(const_loaded, 32)
            dve.wait_ge(turned_out, 4)
            run(dve, body)

        @block.tensor
        def _(pe):
            pe.wait_ge(const_loaded, 32)
            for n in range(3 * NB):
                last = pe.transpose(t_ps[:, n // 4, n % 4, :], picks[:, n].rearrange("p h k -> p (h k)"), ident[:])
            last.then_inc(turned, 1)

            def body(q, s, t0, half, t, first):
                pe.wait_ge(hot_done, q + 1)
                if not first:
                    pe.wait_ge(copied, q - SETS + 1)
                for n in range(SET):
                    last = pe.matmul(ps[:, s, n, :], hot1[:, s, n, :], hot2[:, s, n, :], start=True, stop=True)
                last.then_inc(dense_done, 1)
            run(pe, body)

        @block.scalar
        def _(act):
            act.wait_ge(turned, 1)
            flat = picks_t[:].rearrange("p m t -> p (m t)")
            for n in range(4):
                w = min(4, 3 * NB - 4 * n) * P
                act.activation(flat[:, 512 * n:512 * n + w], t_ps[:, n].rearrange("p a t -> p (a t)")[:, 0:w], ACT.Copy
                               ).then_inc(turned_out, 1)

            def begin(blk, half, first):
                if not first:
                    act.wait_ge(stored[half], 16 * blk)

            def body(q, s, t0, half, t, first):
                act.wait_ge(dense_done, q + 1)
                cols = slice(t, t + SET) if isinstance(t, int) else bass.ds(t, SET)
                act.activation(dense[:, half, :, cols].rearrange("p i t -> p t i"), ps[:, s], ACT.Copy
                               ).then_inc(copied, 1)
            run(act, body, begin)


def experts(nc, io, h_hi, h_lo, x1, gate2):
    GROUPS_E = E_TILES // E_GROUP
    U = E_GROUP
    R = U + KT // 2
    QUAD = 4
    HB = P // 2
    with ExitStack() as ctx:
        sb = lambda n, *shape, dt=F32: ctx.enter_context(nc.sbuf_tensor("e_" + n, [P, *shape], dt))
        sem = lambda n: nc.alloc_semaphore("e_" + n)
        ws = WeightStream(nc, ctx, "we", io["w_experts"])
        gates = sb("gates", 2, 2 * NB, QUAD, HB)
        gelu = sb("gelu", 2, NT)
        a_hi, a_lo = sb("a_hi", E_GROUP, NT, dt=F32R), sb("a_lo", E_GROUP, NT, dt=F32R)
        u_ps = ctx.enter_context(nc.psum_tensor("e_u_ps", [P, 2, 2, 512], F32))
        v_ps = ctx.enter_context(nc.psum_tensor("e_v_ps", [P, 2, 2, 512], F32))
        gates_loaded = [sem("gates0"), sem("gates1")]
        gelu_done, gated, hi_done, lo_done, added = sem("gelu"), sem("gated"), sem("hi"), sem("lo"), sem("added")
        block = ctx.enter_context(nc.Block())

        def run(eng, body):
            body(0, True, False)
            with eng.Fori(1, GROUPS_E - 1) as g:
                body(g, False, False)
            body(GROUPS_E - 1, False, True)

        @block.sync
        def _(sync):
            by_i1 = io["peer_gates"].rearrange("c p i t -> p c i t")

            def load_gates(g, half):
                i2 = E_GROUP * g + QUAD * half
                sync.dma_start(gates[:, half], by_i1[:, :, slice(i2, i2 + QUAD) if isinstance(i2, int)
                                                     else bass.ds(i2, QUAD), :]).then_inc(gates_loaded[half], 16)

            def body(g, first, last):
                if first:
                    for slot in range(2):
                        ws.load(sync, 0, slot)
                    for half in range(2):
                        load_gates(0, half)
                for r in range(1 if first else 0, R):
                    for slot in range(2):
                        ws.load(sync, R * g + r, slot)
                    if r == U and not last:
                        sync.wait_ge(gated, U * g + U)
                        for half in range(2):
                            load_gates(g + 1, half)
            run(sync, body)

        @block.tensor
        def _(pe):
            def body(g, first, last):
                for e in range(U):
                    if e >= 2 or not first:
                        pe.wait_ge(gelu_done, U * g + e - 1)
                    full_product(ws, pe, R * g + e, u_ps[:, e % 2], h_hi, h_lo)
                for n in range(KT):
                    if n == 0:
                        pe.wait_ge(lo_done, U * g + U)
                    if n >= 2 or not first:
                        pe.wait_ge(added, KT * g + n - 1)
                    ws.products(pe, R * g + U + n // 2, n % 2, v_ps[:, n % 2], a_hi, a_lo, 0, True, True)
            run(pe, body)

        @block.scalar
        def _(act):
            def body(g, first, last):
                if first:
                    for slot in range(2):
                        ws.split_hi(act, 0, slot)
                for r in range(R):
                    if not (last and r == R - 1):
                        for slot in range(2):
                            ws.split_hi(act, R * g + r + 1, slot)
                    if r < U:
                        act.wait_ge(ws.used, 2 * (R * g + r) + 2)
                        if r >= 2 or not first:
                            act.wait_ge(lo_done, U * g + r - 1)
                        act.activation(halves(gelu[:, r % 2, :]), u_ps[:, r % 2, :, 0:HALF], ACT.Gelu_apprx_tanh
                                       ).then_inc(gelu_done, 1)
                        act.wait_ge(gated, U * g + r + 1)
                        act.activation(a_hi[:, r, :], gelu[:, r % 2, :], ACT.Copy).then_inc(hi_done, 1)
            run(act, body)

        @block.vector
        def _(dve):
            def body(g, first, last):
                if first:
                    for slot in range(2):
                        ws.split_lo(dve, 0, slot)
                for r in range(R):
                    if not (last and r == R - 1):
                        for slot in range(2):
                            ws.split_lo(dve, R * g + r + 1, slot)
                    if r < U:
                        dve.wait_ge(gates_loaded[r // QUAD], 16 * g + 16)
                        dve.wait_ge(gelu_done, U * g + r + 1)
                        parts = gelu[:, r % 2, :].rearrange("p (c t) -> p c t", t=HB)
                        dve.tensor_tensor(parts, parts, gates[:, r // QUAD, :, r % QUAD, :], ALU.mult).then_inc(gated, 1)
                        dve.wait_ge(hi_done, U * g + r + 1)
                        dve.tensor_tensor(a_lo[:, r, :], gelu[:, r % 2, :], a_hi[:, r, :].bitcast(F32), ALU.subtract
                                          ).then_inc(lo_done, 1)
                    else:
                        for n in (2 * (r - U), 2 * (r - U) + 1):
                            dve.wait_ge(ws.used, 2 * (R * g + U) + n + 1)
                            if not first:
                                dve.wait_ge(added, KT * (g - 1) + n + 1)
                            add_gated(dve, x1[:, n, :], v_ps[:, n % 2], lambda c: gate2[:, n, c:c + 1]
                                      ).then_inc(added, 1)
            run(dve, body)


def phase(build_phase, nc, *args, **kwargs):
    with nc.cleanup_on_exit():
        build_phase(nc, *args, **kwargs)


def program(nc, io):
    with ExitStack() as outer:
        mod = outer.enter_context(nc.sbuf_tensor("mod", [P, 6 * KT, 2], F32))
        tiles = lambda q: mod[:, q * KT:(q + 1) * KT, :]
        shift1, scale1, gate1, shift2, scale2, gate2 = (tiles(q) for q in range(6))
        phase(modulation, nc, io, mod)
        with ExitStack() as ctx:
            h_hi = ctx.enter_context(nc.sbuf_tensor("h_hi", [P, KT, NT], F32R))
            h_lo = ctx.enter_context(nc.sbuf_tensor("h_lo", [P, KT, NT], F32R))
            with nc.sbuf_tensor("x_in", [P, KT, NT], F32) as x:
                phase(norm, nc, io, "n1_", x, io["norm1_g"], scale1, shift1, h_hi, h_lo, x_dram=io["x"])
            with (nc.sbuf_tensor("z_hi", [P, ZT, NT], F32R) as z_hi,
                  nc.sbuf_tensor("z_lo", [P, ZT, NT], F32R) as z_lo):
                phase(conv_branch, nc, io, h_hi, h_lo, z_hi, z_lo)
                phase(gates, nc, io, h_hi, h_lo, z_hi, z_lo)
            phase(project_to_dram, nc, io, "lr", io["w_lora"], 6, io["lora"], h_hi, h_lo,
                            funcs=(ACT.Tanh, ACT.Copy, ACT.Sigmoid))
            phase(project_to_dram, nc, io, "rkv", io["w_rkv"], 3 * NJ, io["rkv"], h_hi, h_lo)
        phase(rwkv, nc, io)
        with ExitStack() as ctx:
            m_hi = ctx.enter_context(nc.sbuf_tensor("m_hi", [P, KT, NT], F32R))
            m_lo = ctx.enter_context(nc.sbuf_tensor("m_lo", [P, KT, NT], F32R))
            with (nc.sbuf_tensor("y_hi", [P, KT, NT], F32R) as y_hi,
                  nc.sbuf_tensor("y_lo", [P, KT, NT], F32R) as y_lo):
                phase(split_y, nc, io, y_hi, y_lo)
                phase(merge, nc, io, y_hi, y_lo, m_hi, m_lo)
            phase(mix, nc, io, m_hi, m_lo, gate1)
        x1 = outer.enter_context(nc.sbuf_tensor("x1", [P, KT, NT], F32))
        peer(nc, io, x1, scale2, shift2, gate2)
        phase(norm, nc, io, "nf_", x1, io["final_g"], None, None, out_dram=io["y"])


def peer(nc, io, x1, scale2, shift2, gate2):
    with (nc.sbuf_tensor("h2_hi", [P, KT, NT], F32R) as h_hi,
          nc.sbuf_tensor("h2_lo", [P, KT, NT], F32R) as h_lo):
        phase(norm, nc, io, "n2_", x1, io["norm2_g"], scale2, shift2, h_hi, h_lo, x_dram=io["x1"])
        with nc.sbuf_tensor("picks", [P, 3 * NB, PEER_HEADS, TOPK], F32) as picks:
            phase(top_experts, nc, io, h_hi, h_lo, picks)
            phase(gate_matrix, nc, io, picks)
        phase(experts, nc, io, h_hi, h_lo, x1, gate2)


def column_tiles(w, k=P):
    K, N = w.shape
    return w.reshape(K // P, P, N // k, k).transpose(2, 1, 0, 3)


def units(t):
    n, p, k, m = t.shape
    return t.reshape(n, p, k // UK, UK * m).transpose(0, 2, 1, 3).reshape(-1, P, UK * P)


def by_channel(v):
    return np.moveaxis(v.reshape(*v.shape[:-1], -1, P), (-1, -2), (0, 1))


def layout(x_prompt, x_sample, state_rwkv, c, c_ctx, w_ada, b_ada, norm1_g, norm2_g, w_in, conv_w,
           w_out_a, w0, w_up, a0, a_up, g_up, k_k, k_a, r_k, ln_g, ln_b, w_o, w_mix, w_q, sub_keys,
           u_tab, v_tab, final_g):
    f = {}
    f["x"] = np.concatenate([x_prompt[0], x_sample[0]]).T.reshape(KT, P, NT)
    f["c_pair"] = by_channel(np.stack([c_ctx, c[0]])).copy()
    f["w_ada"] = column_tiles(w_ada[0]).reshape(6 * KT, P, KT * P)
    f["b_ada"] = by_channel(b_ada[0])
    f["norm1_g"], f["norm2_g"], f["final_g"] = by_channel(norm1_g[0]), by_channel(norm2_g[0]), by_channel(final_g)
    w = w_in[0]
    cuts = np.cumsum([0, D_A, D_A, D_A, D, D, D, LORA, LORA, LORA, LORA, 2 * P, D, D])
    part = [w[:, a:b] for a, b in zip(cuts[:-1], cuts[1:])]
    ub, uc, ux, r, k, v = (units(column_tiles(t)).reshape(-1, 2, P, UK * P) for t in part[:6])
    f["w_conv"] = np.stack([uc, ux, ub], 1).reshape(-1, P, UK * P)
    f["w_rkv"] = np.stack([r, k, v], 1).reshape(-1, P, UK * P)
    ga, gb = (units(column_tiles(t)).reshape(KT // 2, 2, 2, P, UK * P) for t in part[11:13])
    woa = units(column_tiles(w_out_a[0])).reshape(KT // 2, 2, P, UK * P)
    f["w_gates"] = np.concatenate([woa, ga[:, 0], gb[:, 0], ga[:, 1], gb[:, 1]], 1).reshape(-1, P, UK * P)
    lora = [np.pad(t, ((0, 0), (0, P - LORA))) for t in part[6:10]] + [part[10]]
    f["w_lora"] = units(column_tiles(np.concatenate(lora, 1)))
    f["conv_w"] = by_channel(conv_w[0])
    f["ones"] = np.ones((P, P), np.float32)
    f["eps"] = np.tile(np.array([RMS_EPS, GN_EPS, KK_EPS], np.float32), (P, 1))
    i = np.arange(P)
    level = lambda l, rows_late: (((i[:, None] >> (l + 1)) == (i[None] >> (l + 1)))
                                  & (((i[:, None] >> l) & 1) == rows_late) & (((i[None] >> l) & 1) != rows_late))
    masks = [(level(l, 0), level(l, 1)) for l in range(6)] + [(level(0, 1), level(0, 0))]
    f["r_masks"] = np.stack([np.stack(m, 1) for m in masks], 1).astype(np.float32)
    f["ident"] = np.eye(P, dtype=np.float32)
    same = (i[:, None] // 64) == (i[None] // 64)
    before = same & (i[:, None] < i[None])
    both = lambda fwd: np.stack([fwd, fwd.T], 1)
    f["r_causal"] = np.stack([both(before), both(before | np.eye(P, dtype=bool))], 1).astype(np.float32)
    f["r_head_ones"] = np.kron(np.eye(2), np.ones((HEAD, HEAD))).astype(np.float32)
    f["r_keep"] = np.tile((np.arange(NT) % 64 != 0).astype(np.float32), (P, 1))
    vecs = [w0[0, 0], w0[0, 1], a0[0, 0], a0[0, 1], k_k[0], k_a[0], k_a[0], r_k[0].reshape(-1), ln_g[0], ln_b[0]]
    f["r_par"] = np.stack([by_channel(t) for t in vecs], 2)
    low = [np.pad(t[0, d], ((0, P - LORA), (0, 0))) for t in (w_up, a_up) for d in range(2)]
    f["w_low"] = np.stack(low + [g_up[0, :P], g_up[0, P:]], 1).reshape(P, 6, NJ, P).transpose(2, 0, 1, 3)
    f["state"] = state_rwkv[0, 0].reshape(2, NJ, 2, HEAD, HEAD).transpose(1, 2, 4, 0, 3).reshape(NJ, P, 2, HEAD)
    f["w_o"], f["w_mix"], f["w_q"] = (units(column_tiles(t[0])) for t in (w_o, w_mix, w_q))
    f["sub_keys"] = sub_keys[0].transpose(3, 1, 0, 2).reshape(P, 2 * PEER_HEADS, N_KEYS)
    f["iota"] = np.tile(np.arange(P, dtype=np.float32), (P, 1))
    G = E_TILES // E_GROUP
    w = np.empty((G, 2 * E_GROUP + KT, P, UK * P), np.float32)
    w[:, :2 * E_GROUP] = u_tab[0].reshape(P, G, E_GROUP, 2, UK, P).transpose(1, 2, 3, 5, 4, 0).reshape(G, -1, P, UK * P)
    w[:, 2 * E_GROUP:] = v_tab[0].reshape(P, G, E_GROUP, KT, P).transpose(1, 3, 0, 2, 4).reshape(G, KT, P, UK * P)
    f["w_experts"] = w.reshape(-1, P, UK * P)
    return {n: np.ascontiguousarray(a) for n, a in f.items()}


SCRATCH = {"gate_b": (KT, P, NT), "gated_a": (KT, P, NT), "lora": (6, P, NT), "rkv": (3 * NJ, P, NT), "y_b": (NJ, P, NT),
           "x1": (KT, P, NT), "peer_gates": (2 * NB, P, N_KEYS, P // 2)}
OUTPUTS = {"y": (KT, P, NT), "new_state": (NJ, P, 2, HEAD)}


def kernel(**inputs):
    import concourse.bacc as bacc
    from concourse.bass_utils import run_bass_kernel_spmd

    arrays = layout(**{n: np.asarray(a) for n, a in inputs.items()})
    nc = bacc.Bacc("TRN2", target_bir_lowering=False, num_devices=1, dynamic_dma_scratch_size=1024)
    io = {n: nc.dram_tensor("in_" + n, a.shape, mybir.dt.from_np(a.dtype), kind="ExternalInput").ap()
          for n, a in arrays.items()}
    for n, shape in SCRATCH.items():
        io[n] = nc.dram_tensor("s_" + n, shape, F32, kind="Internal").ap()
    for n, shape in OUTPUTS.items():
        io[n] = nc.dram_tensor("out_" + n, shape, F32, kind="ExternalOutput").ap()
    program(nc, io)
    r = run_bass_kernel_spmd(nc, [{"in_" + n: a for n, a in arrays.items()}], core_ids=[0]).results[0]
    y = r["out_y"].reshape(D, NT).T
    state = r["out_new_state"].reshape(NJ, 2, HEAD, 2, HEAD).transpose(3, 0, 1, 4, 2)
    return (np.ascontiguousarray(y[None, :T_PROMPT]), np.ascontiguousarray(y[None, T_PROMPT:]),
            np.ascontiguousarray(state).reshape(1, 1, 2, 2 * NJ, HEAD, HEAD))
```

```python
from contextlib import ExitStack

import numpy as np

import concourse.bass as bass
from concourse import mybir

F32 = mybir.dt.float32
F32R = mybir.dt.float32r
U32 = mybir.dt.uint32
ALU = mybir.AluOpType
ACT = mybir.ActivationFunctionType
AX = mybir.AxisListType

P = 128
D = 2048
KT = D // P
T_PROMPT, T_SAMPLE = 128, 512
NT = T_PROMPT + T_SAMPLE
NB = NT // P
HALF = NT // 2
GRID_W = 64
D_A = 1024
ZT = D_A // P
HEAD = 64
NJ = D // P
LORA = 96
PEER_HEADS = 8
N_KEYS = 128
TOPK = 16
UK = 8
MOD_EARLY = 3 * KT
E_TILES = N_KEYS
E_GROUP = 8
RMS_EPS, GN_EPS, KK_EPS = 1e-6, 64e-5, 1e-12
DECAY_RATE = float(np.exp(-0.5))
GROUPS = ((0, 0, T_PROMPT), (1, T_PROMPT, NT))


def halves(ap):
    return ap.rearrange("p (a n) -> p a n", a=2)


def blocks(ap):
    return ap.rearrange("p (b t) -> p b t", b=NB)


class WeightStream:

    def __init__(self, nc, ctx, name, dram):
        self.dram = dram
        self.raw = ctx.enter_context(nc.sbuf_tensor(name + "_raw", [P, 2, UK * P], F32))
        self.hi = ctx.enter_context(nc.sbuf_tensor(name + "_hi", [P, 2, UK * P], F32R))
        self.lo = ctx.enter_context(nc.sbuf_tensor(name + "_lo", [P, 2, UK * P], F32R))
        self.loaded = [nc.alloc_semaphore(f"{name}_loaded{s}") for s in range(2)]
        self.hi_done = nc.alloc_semaphore(name + "_hi_done")
        self.lo_done = nc.alloc_semaphore(name + "_lo_done")
        self.used = nc.alloc_semaphore(name + "_used")

    def load(self, sync, r, slot):
        if not is_zero(r):
            sync.wait_ge(self.lo_done, 2 * r + slot - 1)
        sync.dma_start(self.raw[:, slot, :], row(self.dram, 2 * r + slot)).then_inc(self.loaded[slot], 16)

    def split_hi(self, act, r, slot):
        act.wait_ge(self.loaded[slot], 16 * r + 16)
        if not is_zero(r):
            act.wait_ge(self.used, 2 * r + slot - 1)
        act.activation(self.hi[:, slot, :], self.raw[:, slot, :], ACT.Copy).then_inc(self.hi_done, 1)

    def split_lo(self, dve, r, slot):
        dve.wait_ge(self.hi_done, 2 * r + slot + 1)
        dve.tensor_tensor(self.lo[:, slot, :], self.raw[:, slot, :], self.hi[:, slot, :].bitcast(F32),
                          ALU.subtract).then_inc(self.lo_done, 1)

    def products(self, pe, r, slot, out, x_hi, x_lo, k0, start, stop, before_last=None):
        pe.wait_ge(self.lo_done, 2 * r + slot + 1)
        for k in range(UK):
            if before_last and k == UK - 1:
                before_last()
            w_hi = self.hi[:, slot, k * P:(k + 1) * P]
            w_lo = self.lo[:, slot, k * P:(k + 1) * P]
            for n, (w, x) in enumerate(((w_hi, x_hi), (w_hi, x_lo), (w_lo, x_hi))):
                for a in range(2):
                    last = pe.matmul(out[:, a, 0:HALF], w, x[:, k0 + k, a * HALF:(a + 1) * HALF],
                                     start=(start and k == 0 and n == 0),
                                     stop=(stop and k == UK - 1 and n == 2))
        last.then_inc(self.used, 1)


def is_zero(i):
    return isinstance(i, int) and i == 0


def at(i):
    return slice(i, i + 1) if isinstance(i, int) else bass.ds(i, 1)


def row(dram, i):
    return dram[i]


def full_product(ws, pe, r, out, x_hi, x_lo):
    ws.products(pe, r, 0, out, x_hi, x_lo, 0, True, False)
    ws.products(pe, r, 1, out, x_hi, x_lo, UK, False, True)


def modulation(nc, io, mod, cond):
    CHUNK, PARTS = 512, 4
    N = MOD_EARLY * P // CHUNK
    TILES = CHUNK // P
    KP = KT // PARTS
    with ExitStack() as ctx:
        sb = lambda name, *shape: ctx.enter_context(nc.sbuf_tensor(name, [P, *shape], F32))
        sem = lambda name: nc.alloc_semaphore(name)
        ada = sb("ada", PARTS, KP * CHUNK)
        sig, padded, ident = sb("cond_sig", KT, 2), sb("cond_padded", KT, P), sb("m_ident", P)
        bias, sums = sb("b_ada", 6 * KT), sb("m_sums", 2, CHUNK)
        ps = ctx.enter_context(nc.psum_tensor("mod_ps", [P, 2, CHUNK], F32))
        turned_ps = ctx.enter_context(nc.psum_tensor("mod_turned", [P, 2, CHUNK], F32))
        small_loaded, sig_done, zeroed = sem("m_small"), sem("m_sig"), sem("m_zeroed")
        ada_loaded = [sem(f"m_ada{s}") for s in range(PARTS)]
        cond_done, part_done, copied, turned, mod_done = (
            sem("m_cond"), sem("m_part"), sem("m_copied"), sem("m_turned"), sem("m_done"))
        block = ctx.enter_context(nc.Block())

        def load_parts(queue, slots):
            for s in slots:
                queue.dma_start(ada[:, s, :], io["w_ada_early"][s]).then_inc(ada_loaded[s], 16)
            with queue.Fori(1, N) as i:
                for s in slots:
                    queue.wait_ge(part_done, PARTS * i + s - 3)
                    queue.dma_start(ada[:, s, :], row(io["w_ada_early"], PARTS * i + s)).then_inc(ada_loaded[s], 16)

        @block.sync
        def _(sync):
            sync.dma_start(cond[:], io["c_pair"]).then_inc(small_loaded, 16)
            sync.dma_start(bias[:], io["b_ada"]).then_inc(small_loaded, 16)
            sync.dma_start(ident[:], io["ident"]).then_inc(small_loaded, 16)
            load_parts(sync, range(PARTS))

        @block.scalar
        def _(act):
            act.wait_ge(small_loaded, 48)
            act.activation(sig[:], cond[:], ACT.Sigmoid).then_inc(sig_done, 1)

            def body(i, bank, first):
                act.wait_ge(part_done, PARTS * i + PARTS)
                if not first:
                    act.wait_ge(turned, i - 1)
                act.activation(sums[:, bank, :], ps[:, bank, :], ACT.Copy).then_inc(copied, 1)
            for i in range(2):
                body(i, i, True)
            with act.Fori(1, N // 2) as i:
                for bank in range(2):
                    body(2 * i + bank, bank, False)

        @block.vector
        def _(dve):
            dve.memset(padded[:], 0.0).then_inc(zeroed, 1)
            dve.wait_ge(small_loaded, 48)
            dve.wait_ge(sig_done, 1)
            dve.tensor_tensor(cond[:], cond[:], sig[:], ALU.mult).then_inc(cond_done, 1)
            dve.wait_ge(cond_done, 1)
            dve.wait_ge(zeroed, 1)
            dve.tensor_copy(padded[:, :, 0:2], cond[:]).then_inc(cond_done, 1)
            with dve.Fori(0, N // 2) as i:
                for bank in range(2):
                    c = 2 * i + bank
                    dve.wait_ge(turned, c + 1)
                    tiles = bass.ds(TILES * c, TILES)
                    dve.tensor_tensor(mod[:, tiles, :],
                                      turned_ps[:, bank, 0:2 * TILES].rearrange("p (m g) -> p m g", g=2),
                                      bias[:, tiles, None].to_broadcast((P, TILES, 2)), ALU.add).then_inc(mod_done, 1)

        @block.tensor
        def _(pe):
            def sums_of(i, bank, first):
                if not first:
                    pe.wait_ge(copied, i - 1)
                for s in range(PARTS):
                    pe.wait_ge(ada_loaded[s], 16 * i + 16)
                    for k in range(KP):
                        last = pe.matmul(ps[:, bank, :], padded[:, KP * s + k, :], ada[:, s, k * CHUNK:(k + 1) * CHUNK],
                                         start=(s == 0 and k == 0), stop=(s == PARTS - 1 and k == KP - 1))
                    last.then_inc(part_done, 1)

            def turn(i, bank, first):
                pe.wait_ge(copied, i + 1)
                if not first:
                    pe.wait_ge(mod_done, i - 1)
                for m in range(TILES):
                    last = pe.matmul(turned_ps[:, bank, 2 * m:2 * m + 2], sums[:, bank, m * P:(m + 1) * P],
                                     ident[:, 0:2], start=True, stop=True)
                last.then_inc(turned, 1)

            pe.wait_ge(cond_done, 2)
            sums_of(0, 0, True)
            sums_of(1, 1, True)
            turn(0, 0, True)
            sums_of(2, 0, False)
            turn(1, 1, True)
            with pe.Fori(1, N // 2 - 1) as i:
                sums_of(2 * i + 1, 1, False)
                turn(2 * i, 0, False)
                sums_of(2 * i + 2, 0, False)
                turn(2 * i + 1, 1, False)
            sums_of(N - 1, 1, False)
            turn(N - 2, 0, False)
            turn(N - 1, 1, False)


def norm(nc, io, name, x, gain, scale, shift, out_hi=None, out_lo=None, x_dram=None, out_dram=None):
    with ExitStack() as ctx:
        sb = lambda n, shape: ctx.enter_context(nc.sbuf_tensor(name + n, shape, F32))
        sem = lambda n: nc.alloc_semaphore(name + n)
        ones, g, amp, eps = sb("ones", [P, P]), sb("gain", [P, KT]), sb("amp", [P, KT, 2]), sb("eps", [P, 3])
        sq, rstd, out = sb("sq", [P, 2, NT]), sb("rstd", [P, NT]), sb("out", [P, 2, NT])
        ps = ctx.enter_context(nc.psum_tensor(name + "ps", [P, 2, 512], F32))
        loaded, squared, summed, rooted = (sem(s) for s in ("ld", "sq_d", "sum", "root"))
        x_loaded = [sem(f"xld{n}") for n in range(KT // 4)]
        amp_done, rstd_done, scaled, shifted, hi_done, lo_done, *stored = (
            sem(s) for s in ("amp_d", "rstd_d", "scaled", "shift", "hi_d", "lo_d", "stored0", "stored1"))
        block = ctx.enter_context(nc.Block())

        @block.sync
        def _(sync):
            sync.dma_start(g[:], gain).then_inc(loaded, 16)
            sync.dma_start(ones[:], io["ones"]).then_inc(loaded, 16)
            sync.dma_start(eps[:], io["eps"]).then_inc(loaded, 16)
            if x_dram is not None:
                for k in range(KT):
                    sync.dma_start(x[:, k, :], x_dram[k]).then_inc(x_loaded[k // 4], 16)
            if out_dram is not None:
                for k in range(KT):
                    sync.wait_ge(shifted, k + 1)
                    sync.dma_start(out_dram[k], out[:, k % 2, :]).then_inc(stored[k % 2], 16)
                for slot in range(2):
                    sync.wait_ge(stored[slot], 16 * (KT // 2))

        @block.scalar
        def _(act):
            for k in range(KT):
                if x_dram is not None:
                    act.wait_ge(x_loaded[k // 4], 16 * 4)
                if k >= 2:
                    act.wait_ge(summed, k - 1)
                act.activation(sq[:, k % 2, :], x[:, k, :], ACT.Square).then_inc(squared, 1)
            act.wait_ge(loaded, 48)
            act.wait_ge(summed, KT)
            act.activation(halves(rstd[:]), ps[:, :, 0:HALF], ACT.Sqrt, scale=1.0 / D,
                           bias=eps[:, 0:1]).then_inc(rooted, 1)
            if out_hi is not None:
                for k in range(KT):
                    act.wait_ge(shifted, 2 * (k + 1))
                    act.activation(out_hi[:, k, :], out[:, k % 2, :], ACT.Copy).then_inc(hi_done, 1)

        @block.tensor
        def _(pe):
            pe.wait_ge(loaded, 48)
            for k in range(KT):
                pe.wait_ge(squared, k + 1)
                for a in range(2):
                    last = pe.matmul(ps[:, a, 0:HALF], ones[:], sq[:, k % 2, a * HALF:(a + 1) * HALF],
                                     start=(k == 0), stop=(k == KT - 1))
                last.then_inc(summed, 1)

        def split_lo(dve, k):
            dve.wait_ge(hi_done, k + 1)
            dve.tensor_tensor(out_lo[:, k, :], out[:, k % 2, :], out_hi[:, k, :].bitcast(F32),
                              ALU.subtract).then_inc(lo_done, 1)

        @block.vector
        def _(dve):
            dve.wait_ge(loaded, 48)
            if scale is not None:
                dve.tensor_scalar(amp[:], scale, 1.0, None, ALU.add).then_inc(amp_done, 1)
                dve.wait_ge(amp_done, 1)
                dve.tensor_tensor(amp[:], amp[:], g[:, :, None].to_broadcast((P, KT, 2)),
                                  ALU.mult).then_inc(amp_done, 1)
                dve.wait_ge(amp_done, 2)
            dve.wait_ge(rooted, 1)
            dve.reciprocal(rstd[:], rstd[:]).then_inc(rstd_done, 1)
            dve.wait_ge(rstd_done, 1)
            for k in range(KT):
                if out_dram is not None:
                    if k >= 2:
                        dve.wait_ge(stored[k % 2], 16 * (k // 2))
                    dve.tensor_tensor(out[:, k % 2, :], x[:, k, :], rstd[:], ALU.mult).then_inc(scaled, 1)
                    dve.wait_ge(scaled, k + 1)
                    dve.tensor_scalar(out[:, k % 2, :], out[:, k % 2, :], g[:, k:k + 1], None,
                                      ALU.mult).then_inc(shifted, 1)
                    continue
                if k >= 2:
                    dve.wait_ge(lo_done, k - 1)
                dve.tensor_tensor(out[:, k % 2, :], x[:, k, :], rstd[:], ALU.mult).then_inc(scaled, 1)
                dve.wait_ge(scaled, k + 1)
                for col, t0, t1 in GROUPS:
                    dve.tensor_scalar(out[:, k % 2, t0:t1], out[:, k % 2, t0:t1], amp[:, k, col:col + 1],
                                      shift[:, k, col:col + 1], ALU.mult, ALU.add).then_inc(shifted, 1)
                if k >= 1:
                    split_lo(dve, k - 1)
            if out_hi is not None:
                split_lo(dve, KT - 1)


def gemm_loop(ws, sync, rounds):
    for slot in range(2):
        ws.load(sync, 0, slot)
    with sync.Fori(1, rounds) as r:
        for slot in range(2):
            ws.load(sync, r, slot)


def conv_branch(nc, io, h_hi, h_lo, z_hi, z_lo):
    with ExitStack() as ctx:
        sb = lambda n, shape: ctx.enter_context(nc.sbuf_tensor(n, shape, F32))
        sem = lambda n: nc.alloc_semaphore(n)
        ws = WeightStream(nc, ctx, "wa", io["w_conv"])
        ps = ctx.enter_context(nc.psum_tensor("a_ps", [P, 3, 2, 512], F32))
        c, z, zc = sb("a_c", [P, NT]), sb("a_z", [P, NT]), sb("a_zc", [P, NT])
        taps = sb("a_taps", [P, ZT, 3])
        taps_loaded, out_done, c_copied = sem("a_taps_l"), sem("a_out"), sem("a_c_d")
        z_done, conv_done, hi_done, lo_done = sem("a_z_d"), sem("a_conv"), sem("a_hi"), sem("a_lo")
        block = ctx.enter_context(nc.Block())

        @block.sync
        def _(sync):
            sync.dma_start(taps[:], io["conv_w"]).then_inc(taps_loaded, 16)
            gemm_loop(ws, sync, 3 * ZT)

        @block.tensor
        def _(pe):
            def body(j, first):
                for s in range(3):
                    if not first:
                        pe.wait_ge(*((c_copied, j), (z_done, j), (conv_done, CONV_STEPS * j))[s])
                    full_product(ws, pe, 3 * j + s, ps[:, s], h_hi, h_lo)
            body(0, True)
            with pe.Fori(1, ZT) as j:
                body(j, False)

        @block.scalar
        def _(act):
            def body(j, first, last):
                for s in range(3):
                    if not (last and s == 2):
                        for slot in range(2):
                            ws.split_hi(act, 3 * j + s + 1, slot)
                    if s == 0:
                        act.wait_ge(ws.used, 6 * j + 2)
                        if not first:
                            act.wait_ge(z_done, j)
                        act.activation(halves(c[:]), ps[:, 0, :, 0:HALF], ACT.Copy).then_inc(c_copied, 1)
                act.wait_ge(conv_done, CONV_STEPS * j + CONV_STEPS)
                act.activation(z_hi[:, at(j), :], zc[:, None, :], ACT.Copy).then_inc(hi_done, 1)
            for slot in range(2):
                ws.split_hi(act, 0, slot)
            body(0, True, False)
            with act.Fori(1, ZT - 1) as j:
                body(j, False, False)
            body(ZT - 1, False, True)

        @block.vector
        def _(dve):
            def body(j, first, last, along_rows):
                for slot in range(2):
                    ws.split_lo(dve, 3 * j + 1, slot)
                for slot in range(2):
                    ws.split_lo(dve, 3 * j + 2, slot)
                dve.wait_ge(c_copied, j + 1)
                dve.wait_ge(ws.used, 6 * j + 4)
                dve.tensor_tensor(halves(z[:]), halves(c[:]), ps[:, 1, :, 0:HALF], ALU.mult
                                  ).then_inc(z_done, 1)
                dve.wait_ge(z_done, j + 1)
                if not first:
                    dve.wait_ge(lo_done, j)
                tap = lambda n: taps[:, at(j), n:n + 1].rearrange("p a n -> p (a n)")
                dve.tensor_scalar(zc[:], z[:], tap(1), None, ALU.mult).then_inc(conv_done, 1)
                step = 1
                for n, dst, src in shifted_views(zc, z, along_rows):
                    dve.wait_ge(conv_done, CONV_STEPS * j + step)
                    dve.scalar_tensor_tensor(dst, src, tap(n), dst, ALU.mult, ALU.add
                                             ).then_inc(conv_done, 1)
                    step += 1
                if not last:
                    for slot in range(2):
                        ws.split_lo(dve, 3 * j + 3, slot)
                dve.wait_ge(conv_done, CONV_STEPS * j + step)
                dve.wait_ge(ws.used, 6 * j + 6)
                dve.tensor_tensor(halves(zc[:]), halves(zc[:]), ps[:, 2, :, 0:HALF], ALU.mult
                                  ).then_inc(conv_done, 1)
                dve.wait_ge(hi_done, j + 1)
                dve.tensor_tensor(z_lo[:, at(j), :], zc[:, None, :], z_hi[:, at(j), :].bitcast(F32),
                                  ALU.subtract).then_inc(lo_done, 1)
            dve.wait_ge(taps_loaded, 16)
            for slot in range(2):
                ws.split_lo(dve, 0, slot)
            body(0, True, False, True)
            with dve.Fori(1, ZT // 2) as j:
                body(j, False, False, True)
            with dve.Fori(ZT // 2, ZT - 1) as j:
                body(j, False, False, False)
            body(ZT - 1, False, True, False)


CONV_STEPS = 6


def shifted_views(zc, z, along_rows):
    p0, s0, n = 0, T_PROMPT, NT
    yield 0, zc[:, p0 + 1:s0], z[:, p0:s0 - 1]
    yield 2, zc[:, p0:s0 - 1], z[:, p0 + 1:s0]
    if along_rows:
        rows = lambda t: t[:, s0:n].rearrange("p (r w) -> p r w", w=GRID_W)
        yield 0, rows(zc)[:, :, 1:GRID_W], rows(z)[:, :, 0:GRID_W - 1]
        yield 2, rows(zc)[:, :, 0:GRID_W - 1], rows(z)[:, :, 1:GRID_W]
    else:
        yield 0, zc[:, s0 + GRID_W:n], z[:, s0:n - GRID_W]
        yield 2, zc[:, s0:n - GRID_W], z[:, s0 + GRID_W:n]


def gates(nc, io, h_hi, h_lo, z_hi, z_lo):
    with ExitStack() as ctx:
        sb = lambda n, shape: ctx.enter_context(nc.sbuf_tensor(n, shape, F32))
        sem = lambda n: nc.alloc_semaphore(n)
        ws = WeightStream(nc, ctx, "wg", io["w_gates"])
        ya_ps = ctx.enter_context(nc.psum_tensor("g_ya", [P, 2, 2, 512], F32))
        gate_ps = ctx.enter_context(nc.psum_tensor("g_ps", [P, 2, 2, 512], F32))
        sig, out_a = sb("g_sig", [P, 4, NT]), sb("g_a", [P, 2, NT])
        sig_done, prod_done, stored_a, stored_b = sem("g_sig_d"), sem("g_prod"), sem("g_sta"), sem("g_stb")
        R = 5
        N = KT // 2
        block = ctx.enter_context(nc.Block())

        @block.sync
        def _(sync):
            gemm_loop(ws, sync, R * N)

        @block.tensor
        def _(pe):
            def body(i, first):
                for s in range(2):
                    if not first:
                        pe.wait_ge(prod_done, 2 * i + s - 1)
                    ws.products(pe, R * i, s, ya_ps[:, s], z_hi, z_lo, 0, True, True)
                for n in range(4):
                    if n >= 2 or not first:
                        pe.wait_ge(sig_done, 4 * i + n - 1)
                    full_product(ws, pe, R * i + 1 + n, gate_ps[:, n % 2], h_hi, h_lo)
            body(0, True)
            with pe.Fori(1, N) as i:
                body(i, False)

        @block.scalar
        def _(act):
            def epilogue(i, n):
                if n == 0:
                    return
                act.wait_ge(ws.used, 2 * (R * i + n) + 2)
                act.activation(halves(sig[:, n - 1, :]), gate_ps[:, (n - 1) % 2, :, 0:HALF], ACT.Sigmoid
                               ).then_inc(sig_done, 1)
                if n in (2, 4):
                    s = n // 2 - 1
                    act.wait_ge(sig_done, 4 * i + n)
                    act.dma_start(row(io["gate_b"], 2 * i + s), sig[:, n - 1, :]).then_inc(stored_b, 16)
                    act.wait_ge(prod_done, 2 * i + s + 1)
                    act.dma_start(row(io["gated_a"], 2 * i + s), out_a[:, s, :]).then_inc(stored_a, 16)

            def body(i, first, last):
                if not first:
                    act.wait_ge(stored_b, 32 * i)
                    act.wait_ge(prod_done, 2 * i)
                for n in range(R):
                    if not (last and n == R - 1):
                        for slot in range(2):
                            ws.split_hi(act, R * i + n + 1, slot)
                    epilogue(i, n)
            for slot in range(2):
                ws.split_hi(act, 0, slot)
            body(0, True, False)
            with act.Fori(1, N - 1) as i:
                body(i, False, False)
            body(N - 1, False, True)
            act.wait_ge(stored_a, 32 * N)
            act.wait_ge(stored_b, 32 * N)

        @block.vector
        def _(dve):
            def body(i, first, last):
                if not first:
                    dve.wait_ge(stored_a, 32 * i)
                for n in range(R):
                    if not (last and n == R - 1):
                        for slot in range(2):
                            ws.split_lo(dve, R * i + n + 1, slot)
                    if n in (2, 4):
                        s = n // 2 - 1
                        dve.wait_ge(sig_done, 4 * i + 2 * s + 1)
                        dve.tensor_tensor(halves(out_a[:, s, :]), halves(sig[:, 2 * s, :]),
                                          ya_ps[:, s, :, 0:HALF], ALU.mult).then_inc(prod_done, 1)
            for slot in range(2):
                ws.split_lo(dve, 0, slot)
            body(0, True, False)
            with dve.Fori(1, N - 1) as i:
                body(i, False, False)
            body(N - 1, False, True)


def project_to_dram(nc, io, name, dram, count, out_dram, x_hi, x_lo, funcs=None, late=None):
    with ExitStack() as ctx:
        sem = lambda n: nc.alloc_semaphore(name + n)
        ws = WeightStream(nc, ctx, name + "_w", dram)
        ps = ctx.enter_context(nc.psum_tensor(name + "_ps", [P, 2, 2, 512], F32))
        out = ctx.enter_context(nc.sbuf_tensor(name + "_out", [P, 2, NT], F32))
        copied, stored = sem("_copied"), [sem(f"_stored{s}") for s in range(2)]
        N = count // 2
        if late:
            mod, cond = late
            assert count == 6 * KT - MOD_EARLY
            ada = ctx.enter_context(nc.sbuf_tensor(name + "_ada", [P, 2, KT * P], F32))
            bias = ctx.enter_context(nc.sbuf_tensor(name + "_b_ada", [P, 6 * KT], F32))
            mod_ps = ctx.enter_context(nc.psum_tensor(name + "_mod_ps", [P, 2, 512], F32))
            bias_loaded, ada_loaded = sem("_bias"), [sem(f"_ada{s}") for s in range(2)]
            tile_done, mod_done = sem("_mod_tile"), sem("_mod_done")
        block = ctx.enter_context(nc.Block())

        @block.sync
        def _(sync):
            def body(i, first):
                for s in range(2):
                    for slot in range(2):
                        ws.load(sync, 2 * i + s, slot)
                    if late:
                        if not first:
                            sync.wait_ge(tile_done, 2 * i + s - 1)
                        sync.dma_start(ada[:, s, :], row(io["w_ada_late"], 2 * i + s)
                                       ).then_inc(ada_loaded[s], 16)
            if late:
                sync.dma_start(bias[:], io["b_ada"]).then_inc(bias_loaded, 16)
            body(0, True)
            with sync.Fori(1, N) as i:
                body(i, False)

        @block.tensor
        def _(pe):
            def body(i, first):
                for s in range(2):
                    if not first:
                        pe.wait_ge(copied, 2 * i + s - 1)
                    full_product(ws, pe, 2 * i + s, ps[:, s], x_hi, x_lo)
                    if late:
                        pe.wait_ge(ada_loaded[s], 16 * i + 16)
                        if not first:
                            pe.wait_ge(mod_done, 2 * i + s - 1)
                        for k in range(KT):
                            last = pe.matmul(mod_ps[:, s, 0:2], ada[:, s, k * P:(k + 1) * P], cond[:, k, :],
                                             start=(k == 0), stop=(k == KT - 1))
                        last.then_inc(tile_done, 1)
            body(0, True)
            with pe.Fori(1, N) as i:
                body(i, False)

        def act_body(act, i, first, last, func):
            for s in range(2):
                if not (last and s):
                    for slot in range(2):
                        ws.split_hi(act, 2 * i + s + 1, slot)
                act.wait_ge(ws.used, 2 * (2 * i + s) + 2)
                if not first:
                    act.wait_ge(stored[s], 16 * i)
                act.activation(halves(out[:, s, :]), ps[:, s, :, 0:HALF], func).then_inc(copied, 1)
                act.wait_ge(copied, 2 * i + s + 1)
                act.dma_start(row(out_dram, 2 * i + s), out[:, s, :]).then_inc(stored[s], 16)

        @block.scalar
        def _(act):
            for slot in range(2):
                ws.split_hi(act, 0, slot)
            if funcs:
                for i in range(N):
                    act_body(act, i, i == 0, i == N - 1, funcs[i])
            else:
                act_body(act, 0, True, False, ACT.Copy)
                with act.Fori(1, N - 1) as i:
                    act_body(act, i, False, False, ACT.Copy)
                act_body(act, N - 1, False, True, ACT.Copy)
            for s in range(2):
                act.wait_ge(stored[s], 16 * N)

        @block.vector
        def _(dve):
            for slot in range(2):
                ws.split_lo(dve, 0, slot)

            def body(i, last):
                for s in range(2):
                    r = 2 * i + s
                    if not (last and s):
                        for slot in range(2):
                            ws.split_lo(dve, r + 1, slot)
                    if late:
                        dve.wait_ge(tile_done, r + 1)
                        m = at(MOD_EARLY + r)
                        dve.tensor_tensor(mod[:, m, :], mod_ps[:, s:s + 1, 0:2],
                                          bias[:, m, None].to_broadcast((P, 1, 2)), ALU.add).then_inc(mod_done, 1)
            if late:
                dve.wait_ge(bias_loaded, 16)
            with dve.Fori(0, N - 1) as i:
                body(i, False)
            body(N - 1, True)



def rwkv(nc, io):
    C = 64
    NC = NT // C
    LEVELS = 6
    NL = (LEVELS - 1) * NB
    STEPS_S = T_SAMPLE // C
    with ExitStack() as ctx:
        def sb(name, *shape, dt=F32):
            return ctx.enter_context(nc.sbuf_tensor("r_" + name, [P, *shape], dt))

        def sem(name):
            return nc.alloc_semaphore("r_" + name)

        masks = sb("masks", LEVELS + 1, 2, P)
        ident = sb("ident", P)
        causal = sb("causal", 2, 2, P)
        head_ones, keep, eps = sb("head_ones", P), sb("keep", NT), sb("eps", 3)
        par = sb("par", NJ, 10)
        low = sb("low", 6, NT)
        rkv, up, st = sb("rkv", 3, NT), sb("up", 6, P), sb("st", 2, 2, HEAD)
        kk, rk, q1 = sb("kk", NT), sb("rk", NT), sb("q1", NT)
        sg, aa, ps_, kd = sb("sg", 2, NT), sb("aa", 2, NT), sb("cum", NT), sb("kd", 2, NT)
        e_l, e_e, e_m = sb("e_l", NT), sb("e_e", NT), sb("e_m", NT)
        th = sb("th", 2, NC)
        t1, t2, t2b, o, cen = q1, e_l, e_e, e_m, kk
        b_t, k_t = sb("b_t", 2, 2, NT), sb("k_t", 2, 2, NT)
        a_t, r_t = sb("a_t", 2, 2, NT), sb("r_t", 2, 2, NT)
        e_h = sb("e_h", 2, 2, NC)
        gate, bonus = sb("gate", 2, NT), sb("bonus", 2, NT)
        v_tok, b_k_tok = sb("v_tok", NB, P), sb("bk_tok", NB, 4, P)
        ka, br, kr, m_t, x, x_t = (sb(n, NB, 4, P) for n in ("ka", "br", "kr", "m_t", "x", "x_t"))
        m_l, mx = sb("m_l", 2, 4, P), sb("mx", 2, 4, P)
        w_u, u = sb("w_u", 2, 4, HEAD), sb("u", NB, 4, HEAD)
        s_in = sb("s_in", STEPS_S + 1, 2, 2, HEAD)
        s_out = sb("s_out", 2, HEAD)
        zeros = sb("zeros", 2 * P, dt=mybir.dt.bfloat16)
        aux = ctx.enter_context(nc.psum_tensor("r_aux", [P, 2, 512], F32))
        bank = ctx.enter_context(nc.psum_tensor("r_bank", [P, 6, 4, P], F32))

        const_loaded, par_done = sem("const"), sem("par")
        in_loaded = sem("in")
        aux_done = {n: sem("aux_" + n) for n in ("wf", "af", "wb", "ab", "gate", "ss", "bonus", "vtok", "mu", "var")}
        low_read = sem("low_read")
        kk_raw, kk_sq, kk_root, kk_inv, kk_done = sem("kk_raw"), sem("kk_sq"), sem("kk_root"), sem("kk_inv"), sem("kk")
        cum, centred, exps = sem("cum"), sem("centred"), sem("exps")
        kd_done, ops_done, rk_done, bonus_done = sem("kd"), sem("ops"), sem("rk"), sem("bonus")
        vtok_done, prod_out, prod_read, bktok_done, x_init = (
            sem("vtok"), sem("prod"), sem("prod_rd"), sem("bktok"), sem("x_init"))
        ml_done, t_out, t_read, d_out, x_add = sem("ml"), sem("t_out"), sem("t_rd"), sem("d_out"), sem("x_add")
        w_out, w_read, u_out, u_read, s_ps = (
            [sem(f"{n}{d}") for d in range(2)] for n in ("w_out", "w_rd", "u_out", "u_rd", "s_ps"))
        s_step = sem("s_step")
        o_out, o_read, cen_done, root2, norm_done, y_done = (
            sem("o_out"), sem("o_rd"), sem("cen"), sem("root2"), sem("normd"), sem("y"))
        y_stored, s_stored, s_final = sem("y_st"), sem("s_st"), sem("s_fin")
        block = ctx.enter_context(nc.Block())

        def chunk_of(d, s, lane):
            first_chunk, n = ((T_PROMPT // C, STEPS_S), (0, T_PROMPT // C))[lane]
            return first_chunk + (s if d == 0 else n - 1 - s)

        lanes = lambda s: (0, 1) if s < T_PROMPT // C else (0,)
        chunks = lambda t: t.rearrange("p (c t) -> p c t", c=NC)
        cols = lambda c: slice(c * P, (c + 1) * P)
        rows = lambda h: slice(h * HEAD, (h + 1) * HEAD)
        by_unit = lambda mask: mask[:, :, None, :].to_broadcast((P, 2, 2, P))
        param = lambda j, n: par[:, at(j), n:n + 1].rearrange("p a n -> p (a n)")
        STEPS = 16
        slot_of = {1 + 3 * k // 2: k for k in range(STEPS)}

        def prepare_pe(pe, k, j, jh, b, first):
            if k < 5:
                name = ("wf", "af", "wb", "ab", "gate")[k]
                if k == 0:
                    pe.wait_ge(in_loaded, 48 * j + 48)
                    if not first:
                        pe.wait_ge(vtok_done, j)
                else:
                    pe.wait_ge(low_read, 5 * j + k)
                for a in range(2):
                    col = slice(a * HALF, (a + 1) * HALF)
                    if k < 4:
                        n = (0, 2, 1, 3)[k]
                        last = pe.matmul(aux[:, a, 0:HALF], up[:, n, :], low[:, n, col], start=True, stop=True)
                    else:
                        for n in (4, 5):
                            last = pe.matmul(aux[:, a, 0:HALF], up[:, n, :], low[:, n, col],
                                             start=(n == 4), stop=(n == 5))
                last.then_inc(aux_done[name], 1)
            if k == 6:
                pe.wait_ge(low_read, 5 * j + 5)
                pe.wait_ge(kk_sq, j + 1)
                sum_heads(pe, t1).then_inc(aux_done["ss"], 1)
            if k == 15:
                pe.wait_ge(kk_root, j + 1)
                pe.wait_ge(rk_done, j + 1)
                sum_heads(pe, rk).then_inc(aux_done["bonus"], 1)

        def sum_heads(pe, src):
            for a in range(2):
                last = pe.matmul(aux[:, a, 0:HALF], head_ones[:], src[:, a * HALF:(a + 1) * HALF],
                                 start=True, stop=True)
            return last

        def prepare_act(act, k, j, jh, b, first):
            if k < 4:
                if k == 0 and not first:
                    act.wait_ge(rk_done, j)
                act.wait_ge(aux_done[("wf", "af", "wb", "ab")[k]], j + 1)
                dst = (sg, aa, sg, aa)[k][:, k // 2, :]
                act.activation(halves(dst), aux[:, :, 0:HALF], ACT.Sigmoid, bias=param(j, (0, 2, 1, 3)[k])
                               ).then_inc(low_read, 1)
            if k == 4:
                act.wait_ge(aux_done["gate"], j + 1)
                act.activation(halves(gate[:, b, :]), aux[:, :, 0:HALF], ACT.Copy).then_inc(low_read, 1)
            if k == 6:
                act.wait_ge(aux_done["ss"], j + 1)
                if not first:
                    act.wait_ge(ops_done, 2 * j)
                act.activation(halves(t2[:]), aux[:, :, 0:HALF], ACT.Sqrt, bias=eps[:, 2:3]).then_inc(kk_root, 1)
            if k in (8, 12):
                d = (k - 8) // 4
                act.wait_ge(centred, 6 * j + 3 * d + 3)
                if not (first and d == 0):
                    act.wait_ge(ops_done, 2 * j + d)
                fwd = ((e_l, ps_, -1), (e_e, q1, -1), (e_m, ps_, 1))
                bwd = ((e_l, q1, 1), (e_e, ps_, 1), (e_m, q1, -1))
                for dst, src, sign in (fwd, bwd)[d]:
                    act.activation(dst[:], src[:], ACT.Exp, scale=sign * DECAY_RATE).then_inc(exps, 1)
                act.activation(e_h[:, b, d, :], th[:, d, :], ACT.Exp, scale=-DECAY_RATE).then_inc(exps, 1)

        def prepare_dve(dve, k, j, jh, b, first):
            r, kx, v = (rkv[:, n, :] for n in range(3))
            if k == 5:
                dve.wait_ge(in_loaded, 48 * j + 48)
                if not isinstance(j, int) or j > 1:
                    dve.wait_ge(y_stored, 16 * (j - 1))
                dve.tensor_scalar(kk[:], kx, param(j, 4), None, ALU.mult).then_inc(kk_raw, 1)
                dve.tensor_scalar(rk[:], r, param(j, 7), None, ALU.mult).then_inc(kk_raw, 1)
                dve.wait_ge(kk_raw, 2 * j + 2)
                dve.tensor_tensor(t1[:], kk[:], kk[:], ALU.mult).then_inc(kk_sq, 1)
            if k == 6:
                dve.wait_ge(kk_root, j + 1)
                dve.reciprocal(t2[:], t2[:]).then_inc(kk_inv, 1)
                dve.wait_ge(kk_inv, j + 1)
                dve.tensor_tensor(kk[:], kk[:], t2[:], ALU.mult).then_inc(kk_done, 1)
            if k in (7, 11):
                d = (k - 7) // 4
                dve.wait_ge(low_read, 5 * j + 3)
                if not (first and d == 0):
                    dve.wait_ge(exps, 8 * j + 4 * d)
                dve.tensor_tensor_scan(ps_[:], keep[:], sg[:, d, :], 0.0, ALU.mult, ALU.add).then_inc(cum, 1)
                dve.wait_ge(cum, 2 * j + d + 1)
                dve.tensor_scalar(th[:, d, :, None], chunks(ps_[:])[:, :, C - 1:C], 0.5, None, ALU.mult
                                  ).then_inc(centred, 1)
                dve.wait_ge(centred, 6 * j + 3 * d + 1)
                dve.tensor_tensor(chunks(ps_[:]), chunks(ps_[:]), th[:, d, :, None].to_broadcast((P, NC, C)),
                                  ALU.subtract).then_inc(centred, 1)
                dve.wait_ge(centred, 6 * j + 3 * d + 2)
                dve.tensor_tensor(q1[:], ps_[:], sg[:, d, :], ALU.subtract).then_inc(centred, 1)
            if k in (8, 12):
                d = (k - 8) // 4
                dve.wait_ge(low_read, 5 * j + 4)
                dve.tensor_scalar(kd[:, d, :], aa[:, d, :], param(j, 5), param(j, 6), ALU.mult, ALU.add
                                  ).then_inc(kd_done, 1)
                dve.wait_ge(kk_done, j + 1)
                dve.tensor_tensor(aa[:, d, :], aa[:, d, :], kk[:], ALU.mult).then_inc(kd_done, 1)
                dve.wait_ge(kd_done, 6 * j + 3 * d + 1)
                dve.tensor_tensor(kd[:, d, :], kd[:, d, :], kx, ALU.mult).then_inc(kd_done, 1)
            if k in (9, 13):
                d = (k - 9) // 4
                dve.wait_ge(exps, 8 * j + 4 * d + 4)
                dve.wait_ge(kd_done, 6 * j + 3 * d + 3)
                dve.tensor_tensor(a_t[:, b, d, :], kk[:], e_e[:], ALU.mult)
                for h in range(2):
                    dve.scalar_tensor_tensor(b_t[rows(h), d, h, :], aa[rows(h), d, :], -1.0, e_m[rows(h), :],
                                             ALU.mult, ALU.mult)
            if k in (10, 14):
                d = (k - 10) // 4
                for h in range(2):
                    dve.tensor_tensor(k_t[rows(h), d, h, :], kd[rows(h), d, :], e_m[rows(h), :], ALU.mult)
                dve.tensor_tensor(r_t[:, b, d, :], r, e_l[:], ALU.mult).then_inc(ops_done, 1)
            if k == 15:
                dve.tensor_tensor(t1[:], kd[:, 0, :], kd[:, 1, :], ALU.add).then_inc(kd_sum, 1)
                dve.wait_ge(kd_sum, j + 1)
                dve.tensor_tensor(rk[:], rk[:], t1[:], ALU.mult).then_inc(rk_done, 1)
                dve.wait_ge(aux_done["bonus"], j + 1)
                dve.tensor_tensor(halves(bonus[:, b, :]), aux[:, :, 0:HALF], halves(v), ALU.mult
                                  ).then_inc(bonus_done, 1)

        kd_sum = sem("kd_sum")

        SSTEP = 2 * STEPS_S
        s_count = lambda j, s, d: SSTEP * j + 2 * s + d + 1
        by_lane = lambda n: bank[:, n].rearrange("p q t -> p (q t)").rearrange("p (l q v) -> p l q v", l=2, v=HEAD)
        of_d = lambda t, d, n: t[:, 0:n, 2 * d:2 * d + 2, :]

        def copy_w(copy, j, s, d):
            n = len(lanes(s))
            copy(of_d(w_u, d, n), of_d(by_lane(d), d, n)).then_inc(w_read[d], 1)

        def copy_u(copy, j, s, d):
            for lane in lanes(s):
                c = chunk_of(d, s, lane)
                half = rows(c % 2)
                last = copy(u[half, c // 2, 2 * d:2 * d + 2, :], by_lane(3 + d)[half, lane, 2 * d:2 * d + 2, :])
            last.then_inc(u_read[d], 1)

        KINDS = 6

        def chunk_pe(pe, j, b, first, last_pair, prep):
            for c in range(NB):
                if c == 0:
                    pe.wait_ge(bonus_done, j + 1)
                    if not first:
                        pe.wait_ge(root2, j)
                last = pe.transpose(aux[:, c // 4, (c % 4) * P:(c % 4 + 1) * P], rkv[:, 2, cols(c)],
                                    ident[:])
            last.then_inc(aux_done["vtok"], 1)
            if not first:
                pe.wait_ge(o_read, j)
                pe.wait_ge(s_step, SSTEP * j)
            at_, rt_ = a_t[:, b], r_t[:, b]
            for c in range(NB):
                of = lambda t, d, h: t[:, d, cols(c)] if t is at_ or t is rt_ else t[:, d, h, cols(c)]
                for n, (lhs, rhs) in enumerate(((k_t, at_), (b_t, rt_), (k_t, rt_), (b_t, at_), (at_, b_t))):
                    if c:
                        pe.wait_ge(prod_read, 5 * (NB * j + c - 1) + n + 1)
                    for q in range(4):
                        d, h = q // 2, q % 2
                        last = pe.matmul(bank[:, n, q, :], of(lhs, d, h), of(rhs, d, h), start=True, stop=True)
                    last.then_inc(prod_out, 1)
                if c:
                    pe.wait_ge(bktok_done, NB * j + c)
                for q in range(4):
                    for h in range(2):
                        src = (b_t, k_t)[q // 2]
                        last = pe.matmul(bank[:, 5, q, rows(h)], src[:, q % 2, h, cols(c)], ident[:, rows(h)],
                                         start=True, stop=True)
                last.then_inc(prod_out, 1)

            def first_product(n):
                c = n % NB
                pe.wait_ge(ml_done, NL * j + n + 1)
                if n < NB:
                    pe.wait_ge(x_init, 2 * (NB * j + c) + 2)
                    if n < 2:
                        pe.wait_ge(prod_read, 5 * (NB * j + NB))
                else:
                    pe.wait_ge(x_add, 2 * (NL * j + n - NB) + 2)
                if n >= 2:
                    pe.wait_ge(t_read, NL * j + n - 1)
                for q in range(4):
                    last = pe.matmul(bank[:, n % 2, q, :], m_l[:, n % 2, q, :], x[:, c, q, :],
                                     start=True, stop=True)
                last.then_inc(t_out, 1)

            def second_products(n):
                c = n % NB
                pe.wait_ge(t_read, NL * j + n + 1)
                if n < 2:
                    pe.wait_ge(bktok_done, NB * j + NB)
                else:
                    pe.wait_ge(x_add, 2 * (NL * j + n - 2) + 2)
                for q in range(4):
                    if n >= NL - NB:
                        break
                    pe.matmul(bank[:, 2 + 2 * (n % 2), q, :], x_t[:, c, q, :], mx[:, n % 2, q, :],
                              start=True, stop=True)
                for q in range(4):
                    last = pe.matmul(bank[:, 3 + 2 * (n % 2), q, :], mx[:, n % 2, q, :], x_t[:, c, q, :],
                                     start=True, stop=True)
                last.then_inc(d_out, 1)

            first_product(0)
            for n in range(NL):
                if n + 1 < NL:
                    first_product(n + 1)
                second_products(n)
                prep(n)
            pe.wait_ge(vtok_done, j + 1)
            pe.wait_ge(x_add, 2 * NL * (j + 1))
            def bound_group(out, n, opens):
                return pe.matmul(out, zeros[:, 0:P], zeros[:, 0:n].rearrange("p (l v) -> p l v", l=out.shape[1]),
                                 start=opens, stop=not opens)

            def w_group(d, s, opens):
                n = len(lanes(s))
                return bound_group(by_lane(d)[:, 0:n, 2 * d:2 * d + 2, :].rearrange("p l q v -> p l (q v)"),
                                   2 * HEAD * n, opens)

            def s_group(d, s, opens):
                n = len(lanes(s))
                return bound_group(bank[:, (2, 5)[d], 0:n, 0:HEAD], HEAD * n, opens)

            def from_v(s):
                for d in range(2):
                    w_group(d, s, True)
                    for lane in lanes(s):
                        for h in range(2):
                            q = 2 * d + h
                            pe.matmul(by_lane(d)[:, lane, q, :], ka[:, chunk_of(d, s, lane) // 2, q, :],
                                      v_tok[:, chunk_of(d, s, lane) // 2, rows(h)], start=False,
                                      stop=False)
            from_v(0)
            for s in range(STEPS_S):
                for d in range(2):
                    pe.wait_ge(s_step, s_count(j, s, d))
                    for lane in lanes(s):
                        if lane == 1 and s == 0:
                            continue
                        for h in range(2):
                            state = s_in[:, s if lane == 0 else STEPS_S, d, h, :]
                            pe.matmul(by_lane(d)[:, lane, 2 * d + h, :],
                                      a_t[:, b, d, cols(chunk_of(d, s, lane) // 2)], state,
                                      start=False, stop=False)
                    w_group(d, s, False).then_inc(w_out[d], 1)
                if s < STEPS_S - 1:
                    for d in range(2):
                        s_group(d, s, True)
                        for lane in lanes(s):
                            c = chunk_of(d, s, lane)
                            half = rows(c % 2)
                            enters = lane == 0 or s > 0
                            for h in range(2):
                                out = bank[rows(h), (2, 5)[d], lane, 0:HEAD]
                                if enters:
                                    pe.matmul(out, ident[:, rows(h)], s_in[:, s if lane == 0 else STEPS_S, d, h, :],
                                              start=False, stop=False)
                                pe.matmul(out, b_k_tok[half, c // 2, 2 + d, rows(h)], v_tok[half, c // 2, rows(h)],
                                          start=False, stop=False)
                for d in range(2):
                    pe.wait_ge(w_read[d], STEPS_S * j + s + 1)
                    for lane in lanes(s):
                        for q in (2 * d, 2 * d + 1):
                            c = chunk_of(d, s, lane) // 2
                            last = pe.matmul(by_lane(3 + d)[:, lane, q, :], x_t[:, c, q, :], w_u[:, lane, q, :],
                                             start=True, stop=True)
                    last.then_inc(u_out[d], 1)
                if s == STEPS_S - 1:
                    continue
                for d in range(2):
                    pe.wait_ge(const_loaded, 16 * 8)
                    pe.wait_ge(u_read[d], STEPS_S * j + s + 1)
                    for lane in lanes(s):
                        c = chunk_of(d, s, lane)
                        half = rows(c % 2)
                        for h in range(2):
                            last = pe.matmul(bank[rows(h), (2, 5)[d], lane, 0:HEAD], b_k_tok[half, c // 2, d, rows(h)],
                                             u[half, c // 2, 2 * d + h, :], start=False, stop=False)
                    s_group(d, s, False).then_inc(s_ps[d], 1)
                from_v(s + 1)
            for d in range(2):
                pe.wait_ge(u_read[d], STEPS_S * (j + 1))
            for c in range(NB):
                for h in range(2):
                    out = bank[rows(h), 3 + c // 4, c % 4, :]
                    for d in range(2):
                        q = 2 * d + h
                        pe.matmul(out, v_tok[:, c, rows(h)], kr[:, c, q, :], start=(d == 0), stop=False)
                        for half in range(2):
                            chunk = 2 * c + half
                            lane = 0 if c else 1
                            s = [s for s in range(STEPS_S) if chunk_of(d, s, lane) == chunk][0]
                            if lane == 1 and s == 0:
                                continue
                            state = s_in[:, s if lane == 0 else STEPS_S, d, h, :]
                            pe.matmul(out[:, half * C:(half + 1) * C], state,
                                      r_t[:, b, d, chunk * C:(chunk + 1) * C], start=False, stop=False)
                        last = pe.matmul(out, u[:, c, q, :], br[:, c, q, :], start=False, stop=(d == 1))
            last.then_inc(o_out, 1)
            pe.wait_ge(o_read, j + 1)
            if not last_pair:
                pe.wait_ge(bonus_done, j + 2)
            sum_heads(pe, o).then_inc(aux_done["mu"], 1)
            pe.wait_ge(cen_done, 2 * j + 2)
            sum_heads(pe, o).then_inc(aux_done["var"], 1)


        def chunk_act(act, j, b, first, last_pair, prep):
            act.wait_ge(aux_done["vtok"], j + 1)
            act.activation(v_tok[:, 0:4, :], aux[:, 0, :].rearrange("p (c t) -> p c t", c=4), ACT.Copy)
            act.activation(v_tok[:, 4, :], aux[:, 1, 0:P], ACT.Copy).then_inc(vtok_done, 1)
            for c in range(NB):
                act.wait_ge(prod_out, KINDS * (NB * j + c + 1))
                act.activation(b_k_tok[:, c], bank[:, 5], ACT.Copy).then_inc(bktok_done, 1)
            for n in range(NL):
                act.wait_ge(t_out, NL * j + n + 1)
                if n >= 2:
                    act.wait_ge(d_out, NL * j + n - 1)
                act.activation(mx[:, n % 2], bank[:, n % 2], ACT.Copy).then_inc(t_read, 1)
                prep(n)
            copy = lambda dst, src: act.activation(dst, src, ACT.Copy)
            for s in range(STEPS_S):
                act.wait_ge(w_out[0], STEPS_S * j + s + 1)
                copy_w(copy, j, s, 0)
                act.wait_ge(u_out[0], STEPS_S * j + s + 1)
                copy_u(copy, j, s, 0)
            act.wait_ge(o_out, j + 1)
            if not first:
                act.wait_ge(cen_done, 2 * j)
            act.activation(o[:, 0:4 * P], bank[:, 3].rearrange("p c t -> p (c t)"), ACT.Copy)
            act.activation(o[:, 4 * P:NT], bank[:, 4, 0, :], ACT.Copy).then_inc(o_read, 1)
            act.wait_ge(aux_done["var"], j + 1)
            act.activation(halves(t2b[:]), aux[:, :, 0:HALF], ACT.Sqrt, scale=1.0 / HEAD, bias=eps[:, 1:2]
                           ).then_inc(root2, 1)

        def chunk_pool(pool, j, b, first):
            level = lambda l: by_unit(masks[:, l])
            units4 = lambda t: t.rearrange("p (d h) n -> p d h n", d=2)
            for c in range(NB):
                pool.wait_ge(prod_read, 5 * (NB * j + c + 1))
                pool.tensor_tensor(x[:, c], x[:, c], ident[:, None, :].to_broadcast((P, 4, P)), ALU.add).then_inc(x_init, 1)
                pool.tensor_tensor(units4(x_t[:, c]), units4(m_t[:, c]), level(0), ALU.mult).then_inc(xt_half, 1)
                pool.wait_ge(xt_half, NB * j + c + 1)
                pool.tensor_tensor(x_t[:, c], x_t[:, c], ident[:, None, :].to_broadcast((P, 4, P)), ALU.add).then_inc(x_init, 1)
                if c < 2:
                    first_masks(pool, j, c, first)
            for n in range(2, NL):
                pool.wait_ge(t_out, NL * j + n - 1)
                pool.tensor_tensor(units4(m_l[:, n % 2]), units4(m_t[:, n % NB]), level(1 + n // NB), ALU.mult
                                   ).then_inc(ml_done, 1)

        def first_masks(pool, j, c, first):
            units4 = lambda t: t.rearrange("p (d h) n -> p d h n", d=2)
            pool.tensor_tensor(units4(m_l[:, c]), units4(m_t[:, c]), by_unit(masks[:, 1]), ALU.mult
                               ).then_inc(ml_done, 1)

        def chunk_dve(dve, j, b, first, last_pair, prep):
            if first:
                dve.memset(s_in[:], 0.0).then_inc(zeroed, 1)
                dve.wait_ge(zeroed, 3)
            units4 = lambda t: t.rearrange("p (d h) n -> p d h n", d=2)
            for c in range(NB):
                for n, (dst, mask) in enumerate(((ka, causal[:, 0]), (br, causal[:, 1]), (kr, causal[:, 1]),
                                                 (m_t, causal[:, 0]), (x, masks[:, LEVELS]))):
                    dve.wait_ge(prod_out, KINDS * (NB * j + c) + n + 1)
                    dve.tensor_tensor(units4(dst[:, c]), units4(bank[:, n]), by_unit(mask), ALU.mult
                                      ).then_inc(prod_read, 1)
            for n in range(NL):
                c = n % NB
                dve.wait_ge(d_out, NL * j + n + 1)
                if n >= NL - NB:
                    dve.tensor_tensor(x_t[:, c], x_t[:, c], bank[:, 3 + 2 * (n % 2)], ALU.add).then_inc(x_add, 2)
                    prep(n)
                    continue
                for t, k in ((x, 2), (x_t, 3)):
                    dve.tensor_tensor(t[:, c], t[:, c], bank[:, k + 2 * (n % 2)], ALU.add).then_inc(x_add, 1)
                prep(n)
            for d in range(2):
                c = chunk_of(d, 0, 0)
                for h in range(2):
                    last = dve.tensor_scalar(s_in[rows(h), 0, d, h, :], st[rows(h), b, d, :],
                                             e_h[rows(h), b, d, c:c + 1], None, ALU.mult)
                last.then_inc(s_step, 1)
            if not first:
                dve.wait_ge(s_stored, 16 * j)
            for s in range(STEPS_S):
                dve.wait_ge(w_out[1], STEPS_S * j + s + 1)
                copy_w(dve.tensor_copy, j, s, 1)
                dve.wait_ge(u_out[1], STEPS_S * j + s + 1)
                copy_u(dve.tensor_copy, j, s, 1)
                if s == STEPS_S - 1:
                    continue
                for d in range(2):
                    dve.wait_ge(s_ps[d], (STEPS_S - 1) * j + s + 1)
                    for lane in lanes(s):
                        c = chunk_of(d, s, lane)
                        if lane == 1 and s == 1:
                            last = dve.tensor_scalar(s_out[:, d, :], bank[:, (2, 5)[d], 1, 0:HEAD],
                                                     e_h[:, b, d, c:c + 1], None, ALU.mult)
                            continue
                        c2 = chunk_of(d, s + 1, lane)
                        for h in range(2):
                            dst = s_in[rows(h), s + 1 if lane == 0 else STEPS_S, d, h, :]
                            last = dve.tensor_scalar(dst, bank[rows(h), (2, 5)[d], lane, 0:HEAD],
                                                     e_h[rows(h), b, d, c:c + 1], e_h[rows(h), b, d, c2:c2 + 1],
                                                     ALU.mult, ALU.mult)
                    last.then_inc(s_step, 1)
            dve.wait_ge(aux_done["mu"], j + 1)
            if last_pair:
                dve.wait_ge(y_stored, 16 * j)
            dve.scalar_tensor_tensor(halves(cen[:]), aux[:, :, 0:HALF], -1.0 / HEAD, halves(o[:]), ALU.mult, ALU.add
                                     ).then_inc(cen_done, 1)
            dve.wait_ge(cen_done, 2 * j + 1)
            dve.tensor_tensor(o[:], cen[:], cen[:], ALU.mult).then_inc(cen_done, 1)
            dve.wait_ge(root2, j + 1)
            dve.reciprocal(t2b[:], t2b[:]).then_inc(norm_done, 1)
            dve.wait_ge(norm_done, 4 * j + 1)
            dve.tensor_tensor(cen[:], cen[:], t2b[:], ALU.mult).then_inc(norm_done, 1)
            dve.wait_ge(norm_done, 4 * j + 2)
            dve.tensor_scalar(cen[:], cen[:], param(j, 8), param(j, 9), ALU.mult, ALU.add).then_inc(norm_done, 1)
            dve.wait_ge(norm_done, 4 * j + 3)
            dve.tensor_tensor(cen[:], cen[:], bonus[:, b, :], ALU.add).then_inc(norm_done, 1)
            dve.wait_ge(norm_done, 4 * j + 4)
            dve.tensor_tensor(cen[:], cen[:], gate[:, b, :], ALU.mult).then_inc(y_done, 1)

        xt_half, zeroed = sem("xt_half"), sem("zeroed")

        def run(eng, prepare, chunk):
            for k in range(STEPS):
                prepare(eng, k, 0, 0, 0, True)

            def body(j, jh, b, first, last):
                def prep(n):
                    if not last and n in slot_of:
                        prepare(eng, slot_of[n], j + 1, jh + b, 1 - b, False)
                chunk(eng, j, b, first, last, prep)
            body(0, 0, 0, True, False)
            with eng.Fori(0, (NJ - 2) // 2) as i:
                body(2 * i + 1, i, 1, False, False)
                body(2 * i + 2, i + 1, 0, False, False)
            body(NJ - 1, (NJ - 1) // 2, 1, False, True)

        @block.tensor
        def _(pe):
            pe.wait_ge(const_loaded, 16 * 8)
            run(pe, prepare_pe, chunk_pe)

        @block.scalar
        def _(act):
            act.wait_ge(const_loaded, 16 * 8)
            run(act, prepare_act, chunk_act)

        @block.vector
        def _(dve):
            dve.wait_ge(const_loaded, 16 * 8)
            dve.tensor_scalar(par[:, :, 6:7], par[:, :, 5:6], -1.0, 1.0, ALU.mult, ALU.add).then_inc(par_done, 1)
            dve.memset(zeros[:], 0.0)
            for t in (b_t, k_t):
                dve.memset(t[:], 0.0).then_inc(zeroed, 1)
            dve.wait_ge(zeroed, 2)
            dve.wait_ge(par_done, 1)
            run(dve, prepare_dve, chunk_dve)

        @block.gpsimd
        def _(pool):
            pool.wait_ge(const_loaded, 16 * 8)
            run(pool, lambda *a: None, lambda eng, j, b, first, last, prep: chunk_pool(eng, j, b, first))

        @block.sync
        def _(sync):
            def load(j, b):
                sync.dma_start(rkv[:], row(io["rkv"].rearrange("(j n) p t -> j p n t", n=3), j)
                               ).then_inc(in_loaded, 16)
                sync.dma_start(up[:], row(io["w_low"], j)).then_inc(in_loaded, 16)
                sync.dma_start(st[:, b], row(io["state"], j)).then_inc(in_loaded, 16)

            for dst, src in ((masks, "r_masks"), (ident, "ident"), (causal, "r_causal"), (head_ones, "r_head_ones"),
                             (keep, "r_keep"), (eps, "eps"), (par, "r_par")):
                sync.dma_start(dst[:], io[src]).then_inc(const_loaded, 16)
            sync.dma_start(low[:], io["lora"].rearrange("n p t -> p n t")).then_inc(const_loaded, 16)
            load(0, 0)

            def body(j, b, last):
                if not last:
                    sync.wait_ge(aux_done["vtok"], j + 1)
                    load(j + 1, 1 - b)
                sync.wait_ge(s_step, s_count(j, 2, 1))
                sync.dma_start(row(io["new_state"], j), s_out[:]).then_inc(s_stored, 16)
                sync.wait_ge(y_done, j + 1)
                sync.dma_start(row(io["y_b"], j), cen[:]).then_inc(y_stored, 16)
            body(0, 0, False)
            with sync.Fori(0, (NJ - 2) // 2) as i:
                body(2 * i + 1, 1, False)
                body(2 * i + 2, 0, False)
            body(NJ - 1, 1, True)
            sync.wait_ge(s_stored, 16 * NJ)
            sync.wait_ge(y_stored, 16 * NJ)


def split_y(nc, io, y_hi, y_lo):
    with ExitStack() as ctx:
        raw = ctx.enter_context(nc.sbuf_tensor("y_raw", [P, 4, NT], F32))
        loaded = [nc.alloc_semaphore(f"y_loaded{s}") for s in range(4)]
        hi_done, lo_done = nc.alloc_semaphore("y_hi_done"), nc.alloc_semaphore("y_lo_done")
        block = ctx.enter_context(nc.Block())

        @block.sync
        def _(sync):
            for j in range(NJ):
                if j >= 4:
                    sync.wait_ge(lo_done, j - 3)
                sync.dma_start(raw[:, j % 4, :], io["y_b"][j]).then_inc(loaded[j % 4], 16)

        @block.scalar
        def _(act):
            for j in range(NJ):
                act.wait_ge(loaded[j % 4], 16 * (j // 4 + 1))
                act.activation(y_hi[:, j, :], raw[:, j % 4, :], ACT.Copy).then_inc(hi_done, 1)

        @block.vector
        def _(dve):
            for j in range(NJ):
                dve.wait_ge(hi_done, j + 1)
                dve.tensor_tensor(y_lo[:, j, :], raw[:, j % 4, :], y_hi[:, j, :].bitcast(F32), ALU.subtract
                                  ).then_inc(lo_done, 1)


def merge(nc, io, y_hi, y_lo, m_hi, m_lo):
    with ExitStack() as ctx:
        sb = lambda n: ctx.enter_context(nc.sbuf_tensor("mg_" + n, [P, 2, NT], F32))
        sem = lambda n: nc.alloc_semaphore("mg_" + n)
        ws = WeightStream(nc, ctx, "wo", io["w_o"])
        ps = ctx.enter_context(nc.psum_tensor("mg_ps", [P, 2, 2, 512], F32))
        gated_a, gate_b = sb("a"), sb("b")
        loaded, gated, summed, hi_done, lo_done = ([sem("l0"), sem("l1")], sem("gated"), sem("sum"), sem("hi"), sem("lo"))
        N = KT // 2
        block = ctx.enter_context(nc.Block())

        @block.sync
        def _(sync):
            def body(i, first):
                for s in range(2):
                    for slot in range(2):
                        ws.load(sync, 2 * i + s, slot)
                    if not first:
                        sync.wait_ge(lo_done, 2 * i + s - 1)
                    sync.dma_start(gated_a[:, s, :], row(io["gated_a"], 2 * i + s)).then_inc(loaded[s], 16)
                    sync.dma_start(gate_b[:, s, :], row(io["gate_b"], 2 * i + s)).then_inc(loaded[s], 16)
            body(0, True)
            with sync.Fori(1, N) as i:
                body(i, False)

        @block.tensor
        def _(pe):
            def body(i, first):
                for s in range(2):
                    if not first:
                        pe.wait_ge(gated, 2 * i + s - 1)
                    full_product(ws, pe, 2 * i + s, ps[:, s], y_hi, y_lo)
            body(0, True)
            with pe.Fori(1, N) as i:
                body(i, False)

        @block.scalar
        def _(act):
            def body(i, last):
                for s in range(2):
                    if not (last and s):
                        for slot in range(2):
                            ws.split_hi(act, 2 * i + s + 1, slot)
                    act.wait_ge(summed, 2 * i + s + 1)
                    act.activation(m_hi[:, at(2 * i + s), :], gate_b[:, s:s + 1, :], ACT.Copy).then_inc(hi_done, 1)
            for slot in range(2):
                ws.split_hi(act, 0, slot)
            with act.Fori(0, N - 1) as i:
                body(i, False)
            body(N - 1, True)

        @block.vector
        def _(dve):
            def body(i, last):
                for s in range(2):
                    if not (last and s):
                        for slot in range(2):
                            ws.split_lo(dve, 2 * i + s + 1, slot)
                    dve.wait_ge(loaded[s], 32 * i + 32)
                    dve.wait_ge(ws.used, 2 * (2 * i + s) + 2)
                    dve.tensor_tensor(halves(gate_b[:, s, :]), halves(gate_b[:, s, :]), ps[:, s, :, 0:HALF],
                                      ALU.mult).then_inc(gated, 1)
                    dve.wait_ge(gated, 2 * i + s + 1)
                    dve.tensor_tensor(gate_b[:, s, :], gate_b[:, s, :], gated_a[:, s, :], ALU.add
                                      ).then_inc(summed, 1)
                    dve.wait_ge(hi_done, 2 * i + s + 1)
                    dve.tensor_tensor(m_lo[:, at(2 * i + s), :], gate_b[:, s:s + 1, :],
                                      m_hi[:, at(2 * i + s), :].bitcast(F32), ALU.subtract).then_inc(lo_done, 1)
            for slot in range(2):
                ws.split_lo(dve, 0, slot)
            with dve.Fori(0, N - 1) as i:
                body(i, False)
            body(N - 1, True)


def add_gated(dve, x, ps, gate):
    for (g, bank, t0, t1) in ((0, 0, 0, T_PROMPT), (1, 0, T_PROMPT, HALF), (1, 1, HALF, NT)):
        last = dve.scalar_tensor_tensor(x[:, t0:t1], ps[:, bank, t0 - bank * HALF:t1 - bank * HALF], gate(g),
                                        x[:, t0:t1], ALU.mult, ALU.add)
    return last


def mix(nc, io, m_hi, m_lo, gate1):
    with ExitStack() as ctx:
        sem = lambda n: nc.alloc_semaphore("mx_" + n)
        ws = WeightStream(nc, ctx, "wm", io["w_mix"])
        ps = ctx.enter_context(nc.psum_tensor("mx_ps", [P, 2, 2, 512], F32))
        x = ctx.enter_context(nc.sbuf_tensor("mx_x", [P, 2, NT], F32))
        loaded, added, stored = [sem("l0"), sem("l1")], sem("added"), [sem("st0"), sem("st1")]
        N = KT // 2
        block = ctx.enter_context(nc.Block())

        @block.sync
        def _(sync):
            def body(i, first):
                for s in range(2):
                    for slot in range(2):
                        ws.load(sync, 2 * i + s, slot)
                    if not first:
                        sync.wait_ge(stored[s], 16 * i)
                    sync.dma_start(x[:, s, :], row(io["x"], 2 * i + s)).then_inc(loaded[s], 16)
            body(0, True)
            with sync.Fori(1, N) as i:
                body(i, False)

        @block.tensor
        def _(pe):
            def body(i, first):
                for s in range(2):
                    if not first:
                        pe.wait_ge(added, 2 * i + s - 1)
                    full_product(ws, pe, 2 * i + s, ps[:, s], m_hi, m_lo)
            body(0, True)
            with pe.Fori(1, N) as i:
                body(i, False)

        @block.scalar
        def _(act):
            def body(i, last):
                for s in range(2):
                    if not (last and s):
                        for slot in range(2):
                            ws.split_hi(act, 2 * i + s + 1, slot)
                    act.wait_ge(added, 2 * i + s + 1)
                    act.dma_start(row(io["x1"], 2 * i + s), x[:, s, :]).then_inc(stored[s], 16)
            for slot in range(2):
                ws.split_hi(act, 0, slot)
            with act.Fori(0, N - 1) as i:
                body(i, False)
            body(N - 1, True)
            for s in range(2):
                act.wait_ge(stored[s], 16 * N)

        @block.vector
        def _(dve):
            def body(i, last):
                for s in range(2):
                    if not (last and s):
                        for slot in range(2):
                            ws.split_lo(dve, 2 * i + s + 1, slot)
                    dve.wait_ge(loaded[s], 16 * i + 16)
                    dve.wait_ge(ws.used, 2 * (2 * i + s) + 2)
                    gate = lambda g: gate1[:, at(2 * i + s), g:g + 1].rearrange("p a n -> p (a n)")
                    add_gated(dve, x[:, s, :], ps[:, s], gate).then_inc(added, 1)
            for slot in range(2):
                ws.split_lo(dve, 0, slot)
            with dve.Fori(0, N - 1) as i:
                body(i, False)
            body(N - 1, True)


def top_experts(nc, io, h_hi, h_lo, picks):
    H = PEER_HEADS
    LOWEST = -3.4e38
    with ExitStack() as ctx:
        sb = lambda n, *shape, dt=F32: ctx.enter_context(nc.sbuf_tensor("t_" + n, [P, *shape], dt))
        sem = lambda n: nc.alloc_semaphore("t_" + n)
        ws = WeightStream(nc, ctx, "wq", io["w_q"])
        keys, iota = sb("keys", 2 * H, N_KEYS), sb("iota", TOPK)
        q, scores, rest = sb("q", 2, NT), sb("scores", 2, NB, N_KEYS), sb("rest", NB, N_KEYS)
        val, idx, idx_f = sb("val", 2, NB, TOPK), sb("idx", 2, NB, TOPK, dt=U32), sb("idx_f", 2, NB, TOPK)
        cand, cand_rest = sb("cand", NB, TOPK * TOPK), sb("cand_rest", NB, TOPK * TOPK)
        top, pos = sb("top", NB, TOPK), sb("pos", NB, TOPK, dt=U32)
        ab, ab_f = sb("ab", 2, NB, TOPK, dt=U32), sb("ab_f", 2, NB, TOPK)
        chosen = sb("chosen", 2, NB * TOPK, TOPK)
        carrier = sb("carrier", TOPK)
        res, total = sb("res", 3, NB, TOPK), sb("total", NB)
        q_ps = ctx.enter_context(nc.psum_tensor("t_q_ps", [P, 2, 2, 512], F32))
        s_ps = ctx.enter_context(nc.psum_tensor("t_s_ps", [P, 2, 1024], F32))
        const_loaded, q_copied, scored, s_copied, ranked = (
            sem("const"), sem("q_copied"), sem("scored"), sem("s_copied"), sem("ranked"))
        step, shifted, exp_done = sem("step"), sem("shifted"), sem("exp")
        block = ctx.enter_context(nc.Block())

        @block.sync
        def _(sync):
            sync.dma_start(keys[:], io["sub_keys"]).then_inc(const_loaded, 16)
            sync.dma_start(iota[:], io["iota"][:, 0:TOPK]).then_inc(const_loaded, 16)
            gemm_loop(ws, sync, 2 * H)

        @block.tensor
        def _(pe):
            def body(i, first):
                for half in range(2):
                    r = 2 * i + half
                    if not first:
                        pe.wait_ge(q_copied, r - 1)
                    full_product(ws, pe, r, q_ps[:, half], h_hi, h_lo)
                    pe.wait_ge(q_copied, r + 1)
                    if not first:
                        pe.wait_ge(s_copied, r - 1)
                    for b in range(NB):
                        last = pe.matmul(s_ps[:, half, b * P:(b + 1) * P], q[:, half, b * P:(b + 1) * P],
                                         keys[:, at(r), :], start=True, stop=True)
                    last.then_inc(scored, 1)
            pe.wait_ge(const_loaded, 32)
            body(0, True)
            with pe.Fori(1, H) as i:
                body(i, False)

        @block.scalar
        def _(act):
            def body(i, first, last):
                for half in range(2):
                    r = 2 * i + half
                    if not (last and half):
                        for slot in range(2):
                            ws.split_hi(act, r + 1, slot)
                    act.wait_ge(ws.used, 2 * r + 2)
                    if not first:
                        act.wait_ge(scored, r - 1)
                    act.activation(halves(q[:, half, :]), q_ps[:, half, :, 0:HALF], ACT.Copy).then_inc(q_copied, 1)
                    act.wait_ge(scored, r + 1)
                    if not first:
                        act.wait_ge(ranked, r - 1)
                    act.activation(scores[:, half], s_ps[:, half, 0:NT].rearrange("p (b t) -> p b t", b=NB), ACT.Copy
                                   ).then_inc(s_copied, 1)
                act.wait_ge(shifted, i + 1)
                act.activation(res[:, 2], top[:], ACT.Exp).then_inc(exp_done, 1)
            for slot in range(2):
                ws.split_hi(act, 0, slot)
            body(0, True, False)
            with act.Fori(1, H - 1) as i:
                body(i, False, False)
            body(H - 1, False, True)

        @block.gpsimd
        def _(pool):
            for slot in range(2):
                ws.split_lo(pool, 0, slot)
            with pool.Fori(1, 2 * H) as r:
                for slot in range(2):
                    ws.split_lo(pool, r, slot)

        @block.vector
        def _(dve):
            STEPS = 20
            def body(i):
                done, used = [0], [0]

                def wait_apart(semaphore, value):
                    dve.wait_ge(semaphore, value)
                    dve.tensor_copy(carrier[:, used[0]:used[0] + 1], iota[:, 0:1])
                    used[0] += 1

                def after_steps():
                    wait_apart(step, STEPS * i + done[0])

                def finish(instruction):
                    done[0] += 1
                    instruction.then_inc(step, 1)

                def rank(v, n, src, left):
                    for b in range(NB):
                        last = dve.max(v[:, b, 0:8], src[:, b, :])
                    finish(last)
                    after_steps()
                    for b in range(NB):
                        dve.max_index(n[:, b, 0:8], v[:, b, 0:8], src[:, b, :])
                    for b in range(NB):
                        last = dve.match_replace(left[:, b, :], v[:, b, 0:8], src[:, b, :], LOWEST)
                    finish(last)
                    after_steps()
                    for b in range(NB):
                        last = dve.max(v[:, b, 8:16], left[:, b, :])
                    finish(last)
                    after_steps()
                    for b in range(NB):
                        last = dve.max_index(n[:, b, 8:16], v[:, b, 8:16], left[:, b, :])
                    return last

                for half in range(2):
                    wait_apart(s_copied, 2 * i + half + 1)
                    rank(val[:, half], idx[:, half], scores[:, half], rest).then_inc(ranked, 1)
                dve.wait_ge(ranked, 2 * i + 2)
                grid = (P, NB, TOPK, TOPK)
                pairs = lambda t: t.rearrange("p b (x y) -> p b x y", x=TOPK)
                finish(dve.tensor_tensor(pairs(cand[:]), val[:, 0, :, :, None].to_broadcast(grid),
                                         val[:, 1, :, None, :].to_broadcast(grid), ALU.add))
                after_steps()
                finish(rank(top, pos, cand, cand_rest))
                dve.wait_ge(step, STEPS * i + done[0])
                dve.tensor_scalar(ab[:, 0], pos[:], 4, None, ALU.logical_shift_right)
                finish(dve.tensor_scalar(ab[:, 1], pos[:], TOPK - 1, None, ALU.bitwise_and))
                finish(dve.tensor_tensor(cand[:, :, 0:TOPK], top[:], top[:, :, 0:1].to_broadcast((P, NB, TOPK)),
                                         ALU.subtract))
                dve.tensor_copy(idx_f[:], idx[:])
                dve.wait_ge(step, STEPS * i + done[0])
                dve.tensor_copy(top[:], cand[:, :, 0:TOPK]).then_inc(shifted, 1)
                finish(dve.tensor_copy(ab_f[:], ab[:]))
                dve.wait_ge(step, STEPS * i + done[0])
                flat = (P, NB * TOPK, TOPK)
                for n in range(2):
                    last = dve.tensor_tensor(chosen[:, n], iota[:, None, :].to_broadcast(flat),
                                             ab_f[:, n].rearrange("p b k -> p (b k)")[:, :, None].to_broadcast(flat),
                                             ALU.is_equal)
                finish(last)
                dve.wait_ge(step, STEPS * i + done[0])
                for n in range(2):
                    view = chosen[:, n].rearrange("p (b k) m -> p b k m", b=NB)
                    last = dve.tensor_tensor(view, view, idx_f[:, n, :, None, :].to_broadcast(grid), ALU.mult)
                finish(last)
                dve.wait_ge(step, STEPS * i + done[0])
                dve.tensor_reduce(res[:, 0:2].rearrange("p n b k -> p (n b k)"),
                                  chosen[:].rearrange("p n s m -> p (n s) m"), AX.X, ALU.add)
                dve.wait_ge(exp_done, i + 1)
                finish(dve.tensor_reduce(total[:], res[:, 2], AX.X, ALU.add))
                dve.wait_ge(step, STEPS * i + done[0])
                finish(dve.reciprocal(total[:], total[:]))
                dve.wait_ge(step, STEPS * i + done[0])
                finish(dve.tensor_tensor(res[:, 2], res[:, 2], total[:, :, None].to_broadcast((P, NB, TOPK)), ALU.mult))
                dve.wait_ge(step, STEPS * i + done[0])
                finish(dve.tensor_copy(picks[:, :, at(i), :], res[:].rearrange("p n b k -> p (n b) k")[:, :, None, :]))
                assert done[0] == STEPS, done
            dve.wait_ge(const_loaded, 32)
            with dve.Fori(0, H) as i:
                body(i)


def gate_matrix(nc, io, picks):
    SET = 4
    SETS = 4
    HB = P // 2
    BODIES = HB // (SET * SETS)
    with ExitStack() as ctx:
        sb = lambda n, *shape: ctx.enter_context(nc.sbuf_tensor("gm_" + n, [P, *shape], F32))
        sem = lambda n: nc.alloc_semaphore("gm_" + n)
        iota, ident = sb("iota", P), sb("ident", P)
        picks_t = sb("picks_t", 3, NT)
        hot = sb("hot", SETS, 2, SET, P)
        dense = sb("dense", 2, N_KEYS, HB)
        ps = ctx.enter_context(nc.psum_tensor("gm_ps", [P, SETS, SET, P], F32))
        t_ps = ctx.enter_context(nc.psum_tensor("gm_t_ps", [P, 4, 4, P], F32))
        const_loaded, turned, turned_out = sem("const"), sem("turned"), sem("turned_out")
        hot_done, weighed, dense_done, copied = sem("hot"), sem("weighed"), sem("dense"), sem("copied")
        stored = [sem("st0"), sem("st1")]
        block = ctx.enter_context(nc.Block())

        def over_sets(eng, body):
            def part(blk, half, k0):
                with eng.Fori(k0, BODIES) as k:
                    for s in range(SETS):
                        t = SET * SETS * k + SET * s
                        body(SETS * BODIES * (2 * blk + half) + SETS * k + s, s, P * blk + HB * half + t, half, t, False)

            def whole(blk, half, first, begin, end):
                begin(blk, half, first)
                if first and half == 0:
                    for s in range(SETS):
                        body(s, s, SET * s, 0, SET * s, True)
                    part(0, 0, 1)
                else:
                    part(blk, half, 0)
                end(blk, half)
            return whole

        def run(eng, body, begin=lambda *a: None, end=lambda *a: None):
            whole = over_sets(eng, body)
            for half in range(2):
                whole(0, half, True, begin, end)
            with eng.Fori(1, NB) as blk:
                for half in range(2):
                    whole(blk, half, False, begin, end)

        @block.sync
        def _(sync):
            sync.dma_start(iota[:], io["iota"]).then_inc(const_loaded, 16)
            sync.dma_start(ident[:], io["ident"]).then_inc(const_loaded, 16)

            def store(blk, half):
                sync.wait_ge(copied, SETS * BODIES * (2 * blk + half + 1))
                sync.dma_start(row(io["peer_gates"], 2 * blk + half), dense[:, half]).then_inc(stored[half], 16)
            for half in range(2):
                store(0, half)
            with sync.Fori(1, NB) as blk:
                for half in range(2):
                    store(blk, half)
            for half in range(2):
                sync.wait_ge(stored[half], 16 * NB)

        token_set = lambda t: slice(t, t + SET) if isinstance(t, int) else bass.ds(t, SET)

        @block.gpsimd
        def _(pool):
            def body(q, s, t0, half, t, first):
                pool.wait_ge(hot_done, q + 1)
                pool.tensor_tensor(hot[:, s, 1], hot[:, s, 1],
                                   picks_t[:, 2, token_set(t0)][:, :, None].to_broadcast((P, SET, P)), ALU.mult
                                   ).then_inc(weighed, 1)
            pool.wait_ge(turned_out, 4)
            run(pool, body)

        @block.vector
        def _(dve):
            def body(q, s, t0, half, t, first):
                if not first:
                    dve.wait_ge(dense_done, q - SETS + 1)
                shape = (P, 2, SET, P)
                dve.tensor_tensor(hot[:, s], iota[:, None, None, :].to_broadcast(shape),
                                  picks_t[:, 0:2, token_set(t0)][:, :, :, None].to_broadcast(shape), ALU.is_equal
                                  ).then_inc(hot_done, 1)
            dve.wait_ge(const_loaded, 32)
            dve.wait_ge(turned_out, 4)
            run(dve, body)

        @block.tensor
        def _(pe):
            pe.wait_ge(const_loaded, 32)
            for n in range(3 * NB):
                last = pe.transpose(t_ps[:, n // 4, n % 4, :], picks[:, n].rearrange("p h k -> p (h k)"), ident[:])
            last.then_inc(turned, 1)

            def body(q, s, t0, half, t, first):
                pe.wait_ge(weighed, q + 1)
                if not first:
                    pe.wait_ge(copied, q - SETS + 1)
                for n in range(SET):
                    last = pe.matmul(ps[:, s, n, :], hot[:, s, 0, n, :], hot[:, s, 1, n, :], start=True, stop=True)
                last.then_inc(dense_done, 1)
            run(pe, body)

        @block.scalar
        def _(act):
            act.wait_ge(turned, 1)
            flat = picks_t[:].rearrange("p m t -> p (m t)")
            for n in range(4):
                w = min(4, 3 * NB - 4 * n) * P
                act.activation(flat[:, 512 * n:512 * n + w], t_ps[:, n].rearrange("p a t -> p (a t)")[:, 0:w], ACT.Copy
                               ).then_inc(turned_out, 1)

            def begin(blk, half, first):
                if not first:
                    act.wait_ge(stored[half], 16 * blk)

            def body(q, s, t0, half, t, first):
                act.wait_ge(dense_done, q + 1)
                act.activation(dense[:, half, :, token_set(t)].rearrange("p i t -> p t i"), ps[:, s], ACT.Copy
                               ).then_inc(copied, 1)
            run(act, body, begin)


def experts(nc, io, h_hi, h_lo, x1, gate2):
    GROUPS_E = E_TILES // E_GROUP
    U = E_GROUP
    R = U + KT // 2
    QUAD = 4
    HB = P // 2
    with ExitStack() as ctx:
        sb = lambda n, *shape, dt=F32: ctx.enter_context(nc.sbuf_tensor("e_" + n, [P, *shape], dt))
        sem = lambda n: nc.alloc_semaphore("e_" + n)
        ws = WeightStream(nc, ctx, "we", io["w_experts"])
        gates = sb("gates", 2, 2 * NB, QUAD, HB)
        gelu = sb("gelu", 2, NT)
        a_hi, a_lo = sb("a_hi", E_GROUP, NT, dt=F32R), sb("a_lo", E_GROUP, NT, dt=F32R)
        u_ps = ctx.enter_context(nc.psum_tensor("e_u_ps", [P, 2, 2, 512], F32))
        v_ps = ctx.enter_context(nc.psum_tensor("e_v_ps", [P, 2, 2, 512], F32))
        gates_loaded = [sem("gates0"), sem("gates1")]
        gelu_done, gated, hi_done, lo_done, added = sem("gelu"), sem("gated"), sem("hi"), sem("lo"), sem("added")
        block = ctx.enter_context(nc.Block())

        def run(eng, body):
            body(0, True, False)
            with eng.Fori(1, GROUPS_E - 1) as g:
                body(g, False, False)
            body(GROUPS_E - 1, False, True)

        @block.sync
        def _(sync):
            by_i1 = io["peer_gates"].rearrange("c p i t -> p c i t")

            def load_gates(g, half):
                i2 = E_GROUP * g + QUAD * half
                sync.dma_start(gates[:, half], by_i1[:, :, slice(i2, i2 + QUAD) if isinstance(i2, int)
                                                     else bass.ds(i2, QUAD), :]).then_inc(gates_loaded[half], 16)

            def body(g, first, last):
                if first:
                    for slot in range(2):
                        ws.load(sync, 0, slot)
                    for half in range(2):
                        load_gates(0, half)
                for r in range(1 if first else 0, R):
                    for slot in range(2):
                        ws.load(sync, R * g + r, slot)
                    if r == U and not last:
                        sync.wait_ge(gated, U * g + U)
                        for half in range(2):
                            load_gates(g + 1, half)
            run(sync, body)

        @block.tensor
        def _(pe):
            def body(g, first, last):
                for e in range(U):
                    if e >= 2 or not first:
                        pe.wait_ge(gelu_done, U * g + e - 1)
                    full_product(ws, pe, R * g + e, u_ps[:, e % 2], h_hi, h_lo)
                for n in range(KT):
                    if n == 0:
                        pe.wait_ge(lo_done, U * g + U - 1)
                    if n >= 2 or not first:
                        pe.wait_ge(added, KT * g + n - 1)
                    ws.products(pe, R * g + U + n // 2, n % 2, v_ps[:, n % 2], a_hi, a_lo, 0, True, True,
                                before_last=(lambda: pe.wait_ge(lo_done, U * g + U)) if n == 0 else None)
            run(pe, body)

        @block.scalar
        def _(act):
            def body(g, first, last):
                if first:
                    for slot in range(2):
                        ws.split_hi(act, 0, slot)
                for r in range(R):
                    if not (last and r == R - 1):
                        for slot in range(2):
                            ws.split_hi(act, R * g + r + 1, slot)
                    if r < U:
                        act.wait_ge(ws.used, 2 * (R * g + r) + 2)
                        if r >= 2 or not first:
                            act.wait_ge(lo_done, U * g + r - 1)
                        act.activation(halves(gelu[:, r % 2, :]), u_ps[:, r % 2, :, 0:HALF], ACT.Gelu_apprx_tanh
                                       ).then_inc(gelu_done, 1)
                        act.wait_ge(gated, U * g + r + 1)
                        act.activation(a_hi[:, r, :], gelu[:, r % 2, :], ACT.Copy).then_inc(hi_done, 1)
            run(act, body)

        @block.vector
        def _(dve):
            def body(g, first, last):
                if first:
                    for slot in range(2):
                        ws.split_lo(dve, 0, slot)
                for r in range(R):
                    for slot in range(2):
                        if not (last and r == R - 1):
                            ws.split_lo(dve, R * g + r + 1, slot)
                        if r >= U:
                            n = 2 * (r - U) + slot
                            dve.wait_ge(ws.used, 2 * (R * g + U) + n + 1)
                            if not first:
                                dve.wait_ge(added, KT * (g - 1) + n + 1)
                            add_gated(dve, x1[:, n, :], v_ps[:, n % 2], lambda c: gate2[:, n, c:c + 1]
                                      ).then_inc(added, 1)
                    if r < U:
                        dve.wait_ge(gates_loaded[r // QUAD], 16 * g + 16)
                        dve.wait_ge(gelu_done, U * g + r + 1)
                        parts = gelu[:, r % 2, :].rearrange("p (c t) -> p c t", t=HB)
                        dve.tensor_tensor(parts, parts, gates[:, r // QUAD, :, r % QUAD, :], ALU.mult).then_inc(gated, 1)
                        dve.wait_ge(hi_done, U * g + r + 1)
                        dve.tensor_tensor(a_lo[:, r, :], gelu[:, r % 2, :], a_hi[:, r, :].bitcast(F32), ALU.subtract
                                          ).then_inc(lo_done, 1)
            run(dve, body)


def phase(build_phase, nc, *args, **kwargs):
    with nc.cleanup_on_exit():
        build_phase(nc, *args, **kwargs)


def program(nc, io):
    with ExitStack() as outer:
        mod = outer.enter_context(nc.sbuf_tensor("mod", [P, 6 * KT, 2], F32))
        tiles = lambda q: mod[:, q * KT:(q + 1) * KT, :]
        shift1, scale1, gate1, shift2, scale2, gate2 = (tiles(q) for q in range(6))
        cond = outer.enter_context(nc.sbuf_tensor("cond", [P, KT, 2], F32))
        phase(modulation, nc, io, mod, cond)
        with ExitStack() as ctx:
            h_hi = ctx.enter_context(nc.sbuf_tensor("h_hi", [P, KT, NT], F32R))
            h_lo = ctx.enter_context(nc.sbuf_tensor("h_lo", [P, KT, NT], F32R))
            with nc.sbuf_tensor("x_in", [P, KT, NT], F32) as x:
                phase(norm, nc, io, "n1_", x, io["norm1_g"], scale1, shift1, h_hi, h_lo, x_dram=io["x"])
            with (nc.sbuf_tensor("z_hi", [P, ZT, NT], F32R) as z_hi,
                  nc.sbuf_tensor("z_lo", [P, ZT, NT], F32R) as z_lo):
                phase(conv_branch, nc, io, h_hi, h_lo, z_hi, z_lo)
                phase(gates, nc, io, h_hi, h_lo, z_hi, z_lo)
            phase(project_to_dram, nc, io, "lr", io["w_lora"], 6, io["lora"], h_hi, h_lo,
                  funcs=(ACT.Tanh, ACT.Copy, ACT.Sigmoid))
            phase(project_to_dram, nc, io, "rkv", io["w_rkv"], 3 * NJ, io["rkv"], h_hi, h_lo,
                  late=(mod, cond))
        phase(rwkv, nc, io)
        with ExitStack() as ctx:
            m_hi = ctx.enter_context(nc.sbuf_tensor("m_hi", [P, KT, NT], F32R))
            m_lo = ctx.enter_context(nc.sbuf_tensor("m_lo", [P, KT, NT], F32R))
            with (nc.sbuf_tensor("y_hi", [P, KT, NT], F32R) as y_hi,
                  nc.sbuf_tensor("y_lo", [P, KT, NT], F32R) as y_lo):
                phase(split_y, nc, io, y_hi, y_lo)
                phase(merge, nc, io, y_hi, y_lo, m_hi, m_lo)
            phase(mix, nc, io, m_hi, m_lo, gate1)
        x1 = outer.enter_context(nc.sbuf_tensor("x1", [P, KT, NT], F32))
        peer(nc, io, x1, scale2, shift2, gate2)
        phase(norm, nc, io, "nf_", x1, io["final_g"], None, None, out_dram=io["y"])


def peer(nc, io, x1, scale2, shift2, gate2):
    with (nc.sbuf_tensor("h2_hi", [P, KT, NT], F32R) as h_hi,
          nc.sbuf_tensor("h2_lo", [P, KT, NT], F32R) as h_lo):
        phase(norm, nc, io, "n2_", x1, io["norm2_g"], scale2, shift2, h_hi, h_lo, x_dram=io["x1"])
        with nc.sbuf_tensor("picks", [P, 3 * NB, PEER_HEADS, TOPK], F32) as picks:
            phase(top_experts, nc, io, h_hi, h_lo, picks)
            phase(gate_matrix, nc, io, picks)
        phase(experts, nc, io, h_hi, h_lo, x1, gate2)


def column_tiles(w, k=P):
    K, N = w.shape
    return w.reshape(K // P, P, N // k, k).transpose(2, 1, 0, 3)


def units(t):
    n, p, k, m = t.shape
    return t.reshape(n, p, k // UK, UK * m).transpose(0, 2, 1, 3).reshape(-1, P, UK * P)


def by_channel(v):
    return np.moveaxis(v.reshape(*v.shape[:-1], -1, P), (-1, -2), (0, 1))


def layout(x_prompt, x_sample, state_rwkv, c, c_ctx, w_ada, b_ada, norm1_g, norm2_g, w_in, conv_w,
           w_out_a, w0, w_up, a0, a_up, g_up, k_k, k_a, r_k, ln_g, ln_b, w_o, w_mix, w_q, sub_keys,
           u_tab, v_tab, final_g):
    f = {}
    f["x"] = np.concatenate([x_prompt[0], x_sample[0]]).T.reshape(KT, P, NT)
    f["c_pair"] = by_channel(np.stack([c_ctx, c[0]])).copy()
    early, late = w_ada[0][:, :MOD_EARLY * P], w_ada[0][:, MOD_EARLY * P:]
    f["w_ada_early"] = column_tiles(early, 512).reshape(-1, P, 4, KT // 4 * 512).transpose(0, 2, 1, 3).reshape(-1, P, KT // 4 * 512)
    f["w_ada_late"] = column_tiles(late).reshape(-1, P, KT * P)
    f["b_ada"] = by_channel(b_ada[0])
    f["norm1_g"], f["norm2_g"], f["final_g"] = by_channel(norm1_g[0]), by_channel(norm2_g[0]), by_channel(final_g)
    w = w_in[0]
    cuts = np.cumsum([0, D_A, D_A, D_A, D, D, D, LORA, LORA, LORA, LORA, 2 * P, D, D])
    part = [w[:, a:b] for a, b in zip(cuts[:-1], cuts[1:])]
    ub, uc, ux, r, k, v = (units(column_tiles(t)).reshape(-1, 2, P, UK * P) for t in part[:6])
    f["w_conv"] = np.stack([uc, ux, ub], 1).reshape(-1, P, UK * P)
    f["w_rkv"] = np.stack([r, k, v], 1).reshape(-1, P, UK * P)
    ga, gb = (units(column_tiles(t)).reshape(KT // 2, 2, 2, P, UK * P) for t in part[11:13])
    woa = units(column_tiles(w_out_a[0])).reshape(KT // 2, 2, P, UK * P)
    f["w_gates"] = np.concatenate([woa, ga[:, 0], gb[:, 0], ga[:, 1], gb[:, 1]], 1).reshape(-1, P, UK * P)
    lora = [np.pad(t, ((0, 0), (0, P - LORA))) for t in part[6:10]] + [part[10]]
    f["w_lora"] = units(column_tiles(np.concatenate(lora, 1)))
    f["conv_w"] = by_channel(conv_w[0])
    f["ones"] = np.ones((P, P), np.float32)
    f["eps"] = np.tile(np.array([RMS_EPS, GN_EPS, KK_EPS], np.float32), (P, 1))
    i = np.arange(P)
    level = lambda l, rows_late: (((i[:, None] >> (l + 1)) == (i[None] >> (l + 1)))
                                  & (((i[:, None] >> l) & 1) == rows_late) & (((i[None] >> l) & 1) != rows_late))
    masks = [(level(l, 0), level(l, 1)) for l in range(6)] + [(level(0, 1), level(0, 0))]
    f["r_masks"] = np.stack([np.stack(m, 1) for m in masks], 1).astype(np.float32)
    f["ident"] = np.eye(P, dtype=np.float32)
    same = (i[:, None] // 64) == (i[None] // 64)
    before = same & (i[:, None] < i[None])
    both = lambda fwd: np.stack([fwd, fwd.T], 1)
    f["r_causal"] = np.stack([both(before), both(before | np.eye(P, dtype=bool))], 1).astype(np.float32)
    f["r_head_ones"] = np.kron(np.eye(2), np.ones((HEAD, HEAD))).astype(np.float32)
    f["r_keep"] = np.tile((np.arange(NT) % 64 != 0).astype(np.float32), (P, 1))
    vecs = [w0[0, 0], w0[0, 1], a0[0, 0], a0[0, 1], k_k[0], k_a[0], k_a[0], r_k[0].reshape(-1), ln_g[0], ln_b[0]]
    f["r_par"] = np.stack([by_channel(t) for t in vecs], 2)
    low = [np.pad(t[0, d], ((0, P - LORA), (0, 0))) for t in (w_up, a_up) for d in range(2)]
    f["w_low"] = np.stack(low + [g_up[0, :P], g_up[0, P:]], 1).reshape(P, 6, NJ, P).transpose(2, 0, 1, 3)
    f["state"] = state_rwkv[0, 0].reshape(2, NJ, 2, HEAD, HEAD).transpose(1, 2, 4, 0, 3).reshape(NJ, P, 2, HEAD)
    f["w_o"], f["w_mix"], f["w_q"] = (units(column_tiles(t[0])) for t in (w_o, w_mix, w_q))
    f["sub_keys"] = sub_keys[0].transpose(3, 1, 0, 2).reshape(P, 2 * PEER_HEADS, N_KEYS)
    f["iota"] = np.tile(np.arange(P, dtype=np.float32), (P, 1))
    G = E_TILES // E_GROUP
    w = np.empty((G, 2 * E_GROUP + KT, P, UK * P), np.float32)
    w[:, :2 * E_GROUP] = u_tab[0].reshape(P, G, E_GROUP, 2, UK, P).transpose(1, 2, 3, 5, 4, 0).reshape(G, -1, P, UK * P)
    w[:, 2 * E_GROUP:] = v_tab[0].reshape(P, G, E_GROUP, KT, P).transpose(1, 3, 0, 2, 4).reshape(G, KT, P, UK * P)
    f["w_experts"] = w.reshape(-1, P, UK * P)
    return {n: np.ascontiguousarray(a) for n, a in f.items()}


SCRATCH = {"gate_b": (KT, P, NT), "gated_a": (KT, P, NT), "lora": (6, P, NT), "rkv": (3 * NJ, P, NT), "y_b": (NJ, P, NT),
           "x1": (KT, P, NT), "peer_gates": (2 * NB, P, N_KEYS, P // 2)}
OUTPUTS = {"y": (KT, P, NT), "new_state": (NJ, P, 2, HEAD)}


def kernel(**inputs):
    import concourse.bacc as bacc
    from concourse.bass_utils import run_bass_kernel_spmd

    arrays = layout(**{n: np.asarray(a) for n, a in inputs.items()})
    nc = bacc.Bacc("TRN2", target_bir_lowering=False, num_devices=1, dynamic_dma_scratch_size=1024)
    io = {n: nc.dram_tensor("in_" + n, a.shape, mybir.dt.from_np(a.dtype), kind="ExternalInput").ap()
          for n, a in arrays.items()}
    for n, shape in SCRATCH.items():
        io[n] = nc.dram_tensor("s_" + n, shape, F32, kind="Internal").ap()
    for n, shape in OUTPUTS.items():
        io[n] = nc.dram_tensor("out_" + n, shape, F32, kind="ExternalOutput").ap()
    program(nc, io)
    r = run_bass_kernel_spmd(nc, [{"in_" + n: a for n, a in arrays.items()}], core_ids=[0]).results[0]
    y = r["out_y"].reshape(D, NT).T
    state = r["out_new_state"].reshape(NJ, 2, HEAD, 2, HEAD).transpose(3, 0, 1, 4, 2)
    return (np.ascontiguousarray(y[None, :T_PROMPT]), np.ascontiguousarray(y[None, T_PROMPT:]),
            np.ascontiguousarray(state).reshape(1, 1, 2, 2 * NJ, HEAD, HEAD))
```
